# Optimizing a Trainium2 kernel written in Bass

```python
import math
import jax, jax.numpy as jnp
from jax import lax
import numpy as np

D_MODEL = 1024
BATCH = 1
SEQ = 1024
DEPTH = 2

N_MIXERS = 2
EXPAND = 2
D_INNER = EXPAND * D_MODEL
POOL_WINDOWS = (2, 4, 8, 16)
N_POOL_GROUPS = len(POOL_WINDOWS)
POOL_GROUP_DIM = D_INNER // N_POOL_GROUPS
SB_HEADS = 16
SB_QK_DIM = 64
SB_V_DIM = D_INNER // SB_HEADS
SB_QK_WIDTH = SB_HEADS * SB_QK_DIM
Q_BLOCK = 128
RMS_EPS = 1e-6
N_POOL_LAYERS = (DEPTH + 1) // 2
N_SB_LAYERS = DEPTH // 2


def rms_norm(x, g):
    x32 = x.astype(jnp.float32)
    inv = lax.rsqrt(jnp.mean(x32 * x32, axis=-1, keepdims=True) + RMS_EPS)
    return (x32 * inv * g.astype(jnp.float32)).astype(x.dtype)

def causal_pool_minus_self(u, window):
    S = u.shape[1]
    u32 = u.astype(jnp.float32)
    c = jnp.cumsum(u32, axis=1)
    c_shift = jnp.pad(c, ((0, 0), (window, 0), (0, 0)))[:, :S]
    count = jnp.minimum(jnp.arange(S) + 1, window).astype(jnp.float32)
    mean = (c - c_shift) / count[None, :, None]
    return (mean - u32).astype(u.dtype)

def pooling_mixer(u, w_in, w_group, scale, w_out):
    B, S, _ = u.shape
    proj = u @ w_in
    xb, z = jnp.split(proj, 2, axis=-1)
    xg = xb.reshape(B, S, N_POOL_GROUPS, POOL_GROUP_DIM)
    pooled = jnp.stack(
        [causal_pool_minus_self(xg[:, :, gi], w) for gi, w in enumerate(POOL_WINDOWS)],
        axis=2)
    mixed = jnp.einsum('bsgi,gio->bsgo', pooled, w_group).reshape(B, S, D_INNER)
    y = mixed * scale * jax.nn.silu(z)
    return y @ w_out

def stick_breaking_attention(q, k, v):
    S = q.shape[2]
    scale = 1.0 / math.sqrt(q.shape[-1])
    n_blocks = S // Q_BLOCK
    outs = []
    for bi in range(n_blocks):
        q_lo = bi * Q_BLOCK
        k_len = q_lo + Q_BLOCK
        qb = q[:, :, q_lo:q_lo + Q_BLOCK].astype(jnp.float32)
        kb = k[:, :, :k_len].astype(jnp.float32)
        vb = v[:, :, :k_len].astype(jnp.float32)
        z = jnp.einsum('bhqd,bhkd->bhqk', qb, kb) * scale
        q_pos = q_lo + jnp.arange(Q_BLOCK)
        k_pos = jnp.arange(k_len)
        mask = k_pos[None, :] < q_pos[:, None]
        log_beta = jax.nn.log_sigmoid(z)
        log_om = jnp.where(mask, jax.nn.log_sigmoid(-z), 0.0)
        later = lax.cumsum(log_om, axis=3, reverse=True) - log_om
        a = jnp.where(mask, jnp.exp(log_beta + later), 0.0)
        outs.append(jnp.einsum('bhqk,bhkd->bhqd', a, vb))
    return jnp.concatenate(outs, axis=2).astype(v.dtype)

def stick_breaking_mixer(u, w_in, w_out):
    B, S, _ = u.shape
    proj = u @ w_in
    q, k, v, z = jnp.split(
        proj, [SB_QK_WIDTH, 2 * SB_QK_WIDTH, 2 * SB_QK_WIDTH + D_INNER], axis=-1)
    q = q.reshape(B, S, SB_HEADS, SB_QK_DIM).transpose(0, 2, 1, 3)
    k = k.reshape(B, S, SB_HEADS, SB_QK_DIM).transpose(0, 2, 1, 3)
    v = v.reshape(B, S, SB_HEADS, SB_V_DIM).transpose(0, 2, 1, 3)
    o = stick_breaking_attention(q, k, v)
    o = o.transpose(0, 2, 1, 3).reshape(B, S, D_INNER)
    y = o * jax.nn.silu(z)
    return y @ w_out

def first_inputs(seed: int = 0) -> dict:
    key = jax.random.key(seed)
    ks = jax.random.split(key, 10)
    f32 = jnp.float32
    x = jax.random.normal(ks[0], (BATCH, SEQ, D_MODEL), f32)
    norm_g = 1.0 + 0.02 * jax.random.normal(ks[1], (DEPTH, D_MODEL), f32)
    pool_w_in = jax.random.normal(ks[2], (N_POOL_LAYERS, D_MODEL, 2 * D_INNER), f32) * D_MODEL ** -0.5
    pool_w = jax.random.normal(ks[3], (N_POOL_LAYERS, N_POOL_GROUPS, POOL_GROUP_DIM, POOL_GROUP_DIM), f32) * POOL_GROUP_DIM ** -0.5
    pool_scale = 1.0 + 0.02 * jax.random.normal(ks[4], (N_POOL_LAYERS, D_INNER), f32)
    pool_w_out = jax.random.normal(ks[5], (N_POOL_LAYERS, D_INNER, D_MODEL), f32) * D_INNER ** -0.5
    sb_w_in = jax.random.normal(ks[6], (N_SB_LAYERS, D_MODEL, 2 * SB_QK_WIDTH + 2 * D_INNER), f32) * D_MODEL ** -0.5
    sb_w_out = jax.random.normal(ks[7], (N_SB_LAYERS, D_INNER, D_MODEL), f32) * D_INNER ** -0.5
    norm_f = 1.0 + 0.02 * jax.random.normal(ks[8], (D_MODEL,), f32)
    return {"x": x, "norm_g": norm_g, "pool_w_in": pool_w_in, "pool_w": pool_w,
            "pool_scale": pool_scale, "pool_w_out": pool_w_out, "sb_w_in": sb_w_in,
            "sb_w_out": sb_w_out, "norm_f": norm_f}

def first_block(x, norm_g, pool_w_in, pool_w, pool_scale, pool_w_out, sb_w_in, sb_w_out, norm_f):
    h = x
    for i in range(DEPTH):
        u = rms_norm(h, norm_g[i])
        j = i // N_MIXERS
        if i % N_MIXERS == 0:
            h = h + pooling_mixer(u, pool_w_in[j], pool_w[j], pool_scale[j], pool_w_out[j])
        else:
            h = h + stick_breaking_mixer(u, sb_w_in[j], sb_w_out[j])
    return rms_norm(h, norm_f)


DEPTH_2 = 1

CHUNK = 64
N_MIXERS_2 = 3
N_LAYERS_A = len(range(0, DEPTH_2, N_MIXERS_2))
N_LAYERS_B = len(range(1, DEPTH_2, N_MIXERS_2))
N_LAYERS_C = len(range(2, DEPTH_2, N_MIXERS_2))
D_FF = 4 * D_MODEL
CONV_W = 4

GDN_DK = 128
GDN_DV = 128
GDN_HEADS = D_MODEL // GDN_DK
GDN_QK = GDN_HEADS * GDN_DK
GDN_V = GDN_HEADS * GDN_DV
GDN_CONV_CH = 2 * GDN_QK + GDN_V
GDN_IN = GDN_CONV_CH + GDN_V + 2 * GDN_HEADS

S5_GROUP = 16
S5_GROUPS = D_MODEL // S5_GROUP
S5_STATE = 64

M2_INNER = 2 * D_MODEL
M2_HEAD_DIM = 64
M2_HEADS = M2_INNER // M2_HEAD_DIM
M2_GROUPS = 8
M2_HPG = M2_HEADS // M2_GROUPS
M2_STATE = 128
M2_BC = M2_GROUPS * M2_STATE
M2_CONV_CH = M2_INNER + 2 * M2_BC
M2_IN = M2_INNER + M2_CONV_CH + M2_HEADS


def rmsnorm(x, g):
    xf = x.astype(jnp.float32)
    y = xf * lax.rsqrt(jnp.mean(xf * xf, axis=-1, keepdims=True) + RMS_EPS)
    return (y * g.astype(jnp.float32)).astype(x.dtype)

def causal_dwconv(x, w):
    return lax.conv_general_dilated(
        x, w[:, None, :], window_strides=(1,), padding=[(w.shape[0] - 1, 0)],
        dimension_numbers=("NWC", "WIO", "NWC"), feature_group_count=x.shape[-1])

def l2norm(t):
    return t * lax.rsqrt(jnp.sum(t * t, axis=-1, keepdims=True) + 1e-6)

def gated_deltanet(h, w_in, conv_w, a_log, dt_bias, o_norm_g, w_out):
    bsz, L, _ = h.shape
    nc = L // CHUNK
    f32 = jnp.float32
    proj = h @ w_in
    qkv, gate, a_raw, b_raw = jnp.split(
        proj, [GDN_CONV_CH, GDN_CONV_CH + GDN_V, GDN_CONV_CH + GDN_V + GDN_HEADS], axis=-1)
    qkv = jax.nn.silu(causal_dwconv(qkv, conv_w)).astype(f32)
    q, k, v = jnp.split(qkv, [GDN_QK, 2 * GDN_QK], axis=-1)
    q = l2norm(q.reshape(bsz, L, GDN_HEADS, GDN_DK)) * (GDN_DK ** -0.5)
    k = l2norm(k.reshape(bsz, L, GDN_HEADS, GDN_DK))
    v = v.reshape(bsz, L, GDN_HEADS, GDN_DV)
    g = -jnp.exp(a_log.astype(f32)) * jax.nn.softplus(a_raw.astype(f32) + dt_bias.astype(f32))
    beta = jax.nn.sigmoid(b_raw.astype(f32))

    def to_chunks(t):
        return t.reshape(bsz, nc, CHUNK, GDN_HEADS, -1).transpose(0, 3, 1, 2, 4)

    qc, kc, vc = to_chunks(q), to_chunks(k), to_chunks(v)
    gc = g.reshape(bsz, nc, CHUNK, GDN_HEADS).transpose(0, 3, 1, 2)
    bc = beta.reshape(bsz, nc, CHUNK, GDN_HEADS).transpose(0, 3, 1, 2)
    G = jnp.cumsum(gc, axis=-1)
    idx = jnp.arange(CHUNK)
    causal = idx[:, None] >= idx[None, :]
    strict = idx[:, None] > idx[None, :]
    decay = jnp.exp(jnp.where(causal, G[..., :, None] - G[..., None, :], -jnp.inf))
    kk = jnp.einsum('bhcid,bhcjd->bhcij', kc, kc)
    tri = jnp.where(strict, bc[..., :, None] * kk * decay, 0.0) + jnp.eye(CHUNK, dtype=f32)
    rhs = jnp.concatenate([vc * bc[..., None], kc * (bc * jnp.exp(G))[..., None]], axis=-1)
    sol = lax.linalg.triangular_solve(tri, rhs, left_side=True, lower=True, unit_diagonal=True)
    u, w = sol[..., :GDN_DV], sol[..., GDN_DV:]
    qk = jnp.einsum('bhcid,bhcjd->bhcij', qc, kc) * decay
    q_dec = qc * jnp.exp(G)[..., None]
    k_dec = kc * jnp.exp(G[..., -1:] - G)[..., None]
    chunk_decay = jnp.exp(G[..., -1])
    xs = tuple(jnp.moveaxis(t, 2, 0) for t in (u, w, qk, q_dec, k_dec, chunk_decay))

    def step(S, inp):
        u_c, w_c, qk_c, qd_c, kd_c, cd_c = inp
        v_new = u_c - jnp.einsum('bhid,bhde->bhie', w_c, S)
        o = jnp.einsum('bhid,bhde->bhie', qd_c, S) + jnp.einsum('bhij,bhje->bhie', qk_c, v_new)
        S = cd_c[..., None, None] * S + jnp.einsum('bhid,bhie->bhde', kd_c, v_new)
        return S, o

    S0 = jnp.zeros((bsz, GDN_HEADS, GDN_DK, GDN_DV), f32)
    _, o = lax.scan(step, S0, xs)
    o = o.transpose(1, 0, 3, 2, 4).reshape(bsz, L, GDN_HEADS, GDN_DV)
    o = rmsnorm(o, o_norm_g) * jax.nn.silu(gate.astype(f32).reshape(bsz, L, GDN_HEADS, GDN_DV))
    return o.reshape(bsz, L, GDN_V).astype(h.dtype) @ w_out

def s5_mixer(h, w_in, lam_re, lam_im, log_dt, b_re, b_im, c_re, c_im, d_skip, w_out):
    bsz, L, _ = h.shape
    f32 = jnp.float32
    u = (h @ w_in).astype(f32)
    ug = u.reshape(bsz, L, S5_GROUPS, S5_GROUP).transpose(1, 0, 2, 3)
    lam = lax.complex(lam_re.astype(f32), lam_im.astype(f32))
    dt = jnp.exp(log_dt.astype(f32))[:, None]
    lam_bar = jnp.exp(lam * dt)
    b_bar = ((lam_bar - 1.0) / lam)[..., None] * lax.complex(b_re.astype(f32), b_im.astype(f32))
    bu = jnp.einsum('gpk,lbgk->lbgp', b_bar, ug.astype(jnp.complex64))
    a = jnp.broadcast_to(lam_bar[None, None], (L, 1, S5_GROUPS, S5_STATE))

    def combine(e1, e2):
        a1, b1 = e1
        a2, b2 = e2
        return a1 * a2, a2 * b1 + b2

    _, states = lax.associative_scan(combine, (a, bu), axis=0)
    c = lax.complex(c_re.astype(f32), c_im.astype(f32))
    y = jnp.real(jnp.einsum('gkp,lbgp->lbgk', c, states)) \
        + d_skip.astype(f32).reshape(S5_GROUPS, S5_GROUP) * ug
    y = jax.nn.gelu(y.transpose(1, 0, 2, 3).reshape(bsz, L, D_MODEL)).astype(h.dtype)
    ag = y @ w_out
    val, gt = jnp.split(ag, 2, axis=-1)
    return val * jax.nn.sigmoid(gt)

def mamba2_mixer(h, w_in, conv_w, conv_b, dt_bias, a_log, d_skip, norm_g, w_out):
    bsz, L, _ = h.shape
    nc = L // CHUNK
    f32 = jnp.float32
    proj = h @ w_in
    z, xbc, dt_raw = jnp.split(proj, [M2_INNER, M2_INNER + M2_CONV_CH], axis=-1)
    xbc = jax.nn.silu(causal_dwconv(xbc, conv_w) + conv_b).astype(f32)
    xs, Bm, Cm = jnp.split(xbc, [M2_INNER, M2_INNER + M2_BC], axis=-1)
    x = xs.reshape(bsz, L, M2_HEADS, M2_HEAD_DIM)
    dt = jax.nn.softplus(dt_raw.astype(f32) + dt_bias.astype(f32))
    dA = dt * (-jnp.exp(a_log.astype(f32)))
    xdt = (x * dt[..., None]).reshape(bsz, nc, CHUNK, M2_GROUPS, M2_HPG, M2_HEAD_DIM)
    Bc = Bm.reshape(bsz, nc, CHUNK, M2_GROUPS, M2_STATE)
    Cc = Cm.reshape(bsz, nc, CHUNK, M2_GROUPS, M2_STATE)
    cum = jnp.cumsum(dA.reshape(bsz, nc, CHUNK, M2_GROUPS, M2_HPG), axis=2)
    idx = jnp.arange(CHUNK)
    causal = (idx[:, None] >= idx[None, :])[:, :, None, None]
    seg = cum[:, :, :, None] - cum[:, :, None, :]
    Lmat = jnp.exp(jnp.where(causal, seg, -jnp.inf))
    cb = jnp.einsum('bclgn,bcsgn->bclsg', Cc, Bc)
    y_diag = jnp.einsum('bclsgr,bcsgrp->bclgrp', cb[..., None] * Lmat, xdt)
    decay_states = jnp.exp(cum[:, :, -1:] - cum)
    states = jnp.einsum('bclgn,bclgrp->bcgrpn', Bc, xdt * decay_states[..., None])
    chunk_decay = jnp.exp(cum[:, :, -1])

    def step(S, inp):
        cd, st = inp
        return cd[..., None, None] * S + st, S

    S0 = jnp.zeros((bsz, M2_GROUPS, M2_HPG, M2_HEAD_DIM, M2_STATE), f32)
    _, S_prev = lax.scan(step, S0, (jnp.moveaxis(chunk_decay, 1, 0), jnp.moveaxis(states, 1, 0)))
    S_prev = jnp.moveaxis(S_prev, 0, 1)
    y_off = jnp.einsum('bclgn,bcgrpn->bclgrp', Cc, S_prev) * jnp.exp(cum)[..., None]
    y = (y_diag + y_off).reshape(bsz, L, M2_HEADS, M2_HEAD_DIM) + d_skip.astype(f32)[:, None] * x
    y = y.reshape(bsz, L, M2_INNER) * jax.nn.silu(z.astype(f32))
    y = rmsnorm(y.reshape(bsz, L, M2_GROUPS, M2_INNER // M2_GROUPS),
                norm_g.reshape(M2_GROUPS, M2_INNER // M2_GROUPS))
    return y.reshape(bsz, L, M2_INNER).astype(h.dtype) @ w_out

def sq_relu_mlp(h, w1, w2):
    return jnp.square(jax.nn.relu(h @ w1)) @ w2

def _inv_softplus_dt(key, shape):
    dt = jnp.exp(jax.random.uniform(key, shape, minval=math.log(1e-3), maxval=math.log(1e-1)))
    return dt + jnp.log(-jnp.expm1(-dt))

def second_inputs(seed: int = 0) -> dict:
    key = jax.random.key(seed)
    ks = jax.random.split(key, 32)
    nrm = jax.random.normal
    f32 = jnp.float32
    nA, nB, nC = N_LAYERS_A, N_LAYERS_B, N_LAYERS_C
    return {
        "x": nrm(ks[0], (BATCH, SEQ, D_MODEL), f32),
        "norm_mix_g": 1.0 + 0.02 * nrm(ks[1], (DEPTH_2, D_MODEL), f32),
        "norm_mlp_g": 1.0 + 0.02 * nrm(ks[2], (DEPTH_2, D_MODEL), f32),
        "mlp_w1": nrm(ks[3], (DEPTH_2, D_MODEL, D_FF), f32) * D_MODEL ** -0.5,
        "mlp_w2": nrm(ks[4], (DEPTH_2, D_FF, D_MODEL), f32) * D_FF ** -0.5,
        "gdn_w_in": nrm(ks[5], (nA, D_MODEL, GDN_IN), f32) * D_MODEL ** -0.5,
        "gdn_conv_w": nrm(ks[6], (nA, CONV_W, GDN_CONV_CH), f32) * CONV_W ** -0.5,
        "gdn_a_log": jnp.log(jax.random.uniform(ks[7], (nA, GDN_HEADS), minval=1.0, maxval=16.0)),
        "gdn_dt_bias": _inv_softplus_dt(ks[8], (nA, GDN_HEADS)),
        "gdn_o_norm_g": 1.0 + 0.02 * nrm(ks[9], (nA, GDN_DV), f32),
        "gdn_w_out": nrm(ks[10], (nA, GDN_V, D_MODEL), f32) * GDN_V ** -0.5,
        "s5_w_in": nrm(ks[11], (nB, D_MODEL, D_MODEL), f32) * D_MODEL ** -0.5,
        "s5_lam_re": -0.5 + 0.01 * nrm(ks[12], (nB, S5_GROUPS, S5_STATE), f32),
        "s5_lam_im": math.pi * jnp.arange(S5_STATE, dtype=f32) + 0.01 * nrm(ks[13], (nB, S5_GROUPS, S5_STATE), f32),
        "s5_log_dt": jax.random.uniform(ks[14], (nB, S5_GROUPS), minval=math.log(1e-3), maxval=math.log(1e-1)),
        "s5_b_re": nrm(ks[15], (nB, S5_GROUPS, S5_STATE, S5_GROUP), f32) * (2 * S5_GROUP) ** -0.5,
        "s5_b_im": nrm(ks[16], (nB, S5_GROUPS, S5_STATE, S5_GROUP), f32) * (2 * S5_GROUP) ** -0.5,
        "s5_c_re": nrm(ks[17], (nB, S5_GROUPS, S5_GROUP, S5_STATE), f32) * (2 * S5_STATE) ** -0.5 * 4.0,
        "s5_c_im": nrm(ks[18], (nB, S5_GROUPS, S5_GROUP, S5_STATE), f32) * (2 * S5_STATE) ** -0.5 * 4.0,
        "s5_d": nrm(ks[19], (nB, D_MODEL), f32),
        "s5_w_out": nrm(ks[20], (nB, D_MODEL, 2 * D_MODEL), f32) * D_MODEL ** -0.5,
        "m2_w_in": nrm(ks[21], (nC, D_MODEL, M2_IN), f32) * D_MODEL ** -0.5,
        "m2_conv_w": nrm(ks[22], (nC, CONV_W, M2_CONV_CH), f32) * CONV_W ** -0.5,
        "m2_conv_b": 0.02 * nrm(ks[23], (nC, M2_CONV_CH), f32),
        "m2_dt_bias": _inv_softplus_dt(ks[24], (nC, M2_HEADS)),
        "m2_a_log": jnp.log(jax.random.uniform(ks[25], (nC, M2_HEADS), minval=1.0, maxval=16.0)),
        "m2_d": 1.0 + 0.02 * nrm(ks[26], (nC, M2_HEADS), f32),
        "m2_norm_g": 1.0 + 0.02 * nrm(ks[27], (nC, M2_INNER), f32),
        "m2_w_out": nrm(ks[28], (nC, M2_INNER, D_MODEL), f32) * M2_INNER ** -0.5,
        "final_norm_g": 1.0 + 0.02 * nrm(ks[29], (D_MODEL,), f32),
    }

def second_block(x, norm_mix_g, norm_mlp_g, mlp_w1, mlp_w2,
              gdn_w_in, gdn_conv_w, gdn_a_log, gdn_dt_bias, gdn_o_norm_g, gdn_w_out,
              s5_w_in, s5_lam_re, s5_lam_im, s5_log_dt, s5_b_re, s5_b_im, s5_c_re, s5_c_im, s5_d, s5_w_out,
              m2_w_in, m2_conv_w, m2_conv_b, m2_dt_bias, m2_a_log, m2_d, m2_norm_g, m2_w_out,
              final_norm_g):
    h = x
    for i in range(DEPTH_2):
        kind, j = i % N_MIXERS_2, i // N_MIXERS_2
        hn = rmsnorm(h, norm_mix_g[i])
        if kind == 0:
            m = gated_deltanet(hn, gdn_w_in[j], gdn_conv_w[j], gdn_a_log[j], gdn_dt_bias[j],
                               gdn_o_norm_g[j], gdn_w_out[j])
        elif kind == 1:
            m = s5_mixer(hn, s5_w_in[j], s5_lam_re[j], s5_lam_im[j], s5_log_dt[j], s5_b_re[j],
                         s5_b_im[j], s5_c_re[j], s5_c_im[j], s5_d[j], s5_w_out[j])
        else:
            m = mamba2_mixer(hn, m2_w_in[j], m2_conv_w[j], m2_conv_b[j], m2_dt_bias[j], m2_a_log[j],
                             m2_d[j], m2_norm_g[j], m2_w_out[j])
        h = h + m.astype(h.dtype)
        h = h + sq_relu_mlp(rmsnorm(h, norm_mlp_g[i]), mlp_w1[i], mlp_w2[i]).astype(h.dtype)
    return rmsnorm(h, final_norm_g)


def setup_inputs(seed=0):
    out = dict(first_inputs(seed))
    for name, value in second_inputs(seed + 1).items():
        if name != "x":
            out[name + "_2"] = value
    return out


def reference(
    x, norm_g, pool_w_in, pool_w, pool_scale, pool_w_out, sb_w_in, sb_w_out, norm_f,
    norm_mix_g_2, norm_mlp_g_2, mlp_w1_2, mlp_w2_2, gdn_w_in_2, gdn_conv_w_2, gdn_a_log_2,
    gdn_dt_bias_2, gdn_o_norm_g_2, gdn_w_out_2, s5_w_in_2, s5_lam_re_2, s5_lam_im_2,
    s5_log_dt_2, s5_b_re_2, s5_b_im_2, s5_c_re_2, s5_c_im_2, s5_d_2, s5_w_out_2, m2_w_in_2,
    m2_conv_w_2, m2_conv_b_2, m2_dt_bias_2, m2_a_log_2, m2_d_2, m2_norm_g_2, m2_w_out_2,
    final_norm_g_2,
):
    x = first_block(
        x, norm_g, pool_w_in, pool_w, pool_scale, pool_w_out, sb_w_in, sb_w_out, norm_f,
    )
    return second_block(
        x, norm_mix_g_2, norm_mlp_g_2, mlp_w1_2, mlp_w2_2, gdn_w_in_2, gdn_conv_w_2,
        gdn_a_log_2, gdn_dt_bias_2, gdn_o_norm_g_2, gdn_w_out_2, s5_w_in_2, s5_lam_re_2,
        s5_lam_im_2, s5_log_dt_2, s5_b_re_2, s5_b_im_2, s5_c_re_2, s5_c_im_2, s5_d_2,
        s5_w_out_2, m2_w_in_2, m2_conv_w_2, m2_conv_b_2, m2_dt_bias_2, m2_a_log_2, m2_d_2,
        m2_norm_g_2, m2_w_out_2, final_norm_g_2,
    )


_drawn_inputs = setup_inputs


def setup_inputs(seed=0):
    import zlib

    import numpy as np

    out = dict(_drawn_inputs(seed))
    spreads = {}
    factors = {'pool_scale': 4.441,
     'norm_mix_g_2': 3.075,
     'norm_mlp_g_2': 11.326,
     'gdn_o_norm_g_2': 17.82,
     'final_norm_g_2': 7.672}
    for name, (base, spread) in spreads.items():
        noise = np.random.default_rng([zlib.crc32(name.encode()), seed]).standard_normal(out[name].shape)
        drawn = base * np.exp(spread * noise) if base else spread * noise
        out[name] = __import__('jax').numpy.asarray(drawn.astype(out[name].dtype))
    for name, factor in factors.items():
        out[name] = (out[name] * factor).astype(out[name].dtype)
    return out
```

```python
from contextlib import ExitStack

import numpy as np

import concourse.bass as bass
from concourse import mybir

F32 = mybir.dt.float32
F32R = mybir.dt.float32r
ALU = mybir.AluOpType
ACT = mybir.ActivationFunctionType
AX = mybir.AxisListType

S = 1024
D = 1024
KT = 8
EPS = 1e-6
KB = 1024


class Queue:

    def __init__(self, engine, sem):
        self.engine, self.sem, self.count, self.seen = engine, sem, 0, {}

    def wait(self, *after):
        for sem, n in after:
            if self.seen.get(sem, 0) < n:
                self.seen[sem] = n
                self.engine.wait_ge(sem, n)

    def do(self, fn, *after, mark=True):
        self.wait(*after)
        ins = fn(self.engine)
        if mark:
            ins.then_inc(self.sem, 1)
            self.count += 1
        return self.sem, self.count


class Loader(Queue):

    def __init__(self, engine):
        super().__init__(engine, None)
        self.counts = {}

    def dma(self, dst, src, sem, *after):
        self.wait(*after)
        self.engine.dma_start(dst.bitcast(F32), src.bitcast(F32)).then_inc(sem, 16)
        self.counts[sem] = self.counts.get(sem, 0) + 16
        return sem, self.counts[sem]


class Slots:

    def __init__(self, bufs, free=()):
        self.line = [(b, list(free)) for b in bufs]

    def take(self):
        return self.line.pop(0)

    def put(self, buf, *tokens):
        self.line.append((buf, list(tokens)))


def program(nc, A, out, upto=99):
    ctx = ExitStack()
    with ctx:
        base = (nc.sbuf_base + 31) // 32 * 32
        arena = ctx.enter_context(nc.sbuf_tensor("arena", [128, 53200], F32))
        names = [0]

        def at(kb, shape, dt=F32):
            names[0] += 1
            return nc.alloc_sbuf_tensor_at(f"m{names[0]}", [128] + shape, dt,
                                           offset=base + int(kb * KB))

        def sem(name):
            return ctx.enter_context(nc.semaphore(name))

        pe = Queue(nc.tensor, sem("pe"))
        dve = Queue(nc.vector, sem("dve"))
        act = Queue(nc.scalar, sem("act"))
        pool = Queue(nc.gpsimd, sem("pool"))
        sp = Loader(nc.sync)

        psum = [ctx.enter_context(nc.psum_tensor(f"ps{i}", [128, 1024], F32)) for i in range(4)]
        PSW = Slots(psum)

        H = at(0, [KT, S])
        UH = at(32, [KT, S], F32R)
        UL = at(64, [KT, S], F32R)
        STG = [at(96 + 4 * i, [1024]) for i in range(3)]
        WH = [at(108 + 8 * i, [1024], F32R) for i in range(3)]
        WL = [at(112 + 8 * i, [1024], F32R) for i in range(3)]
        INV = at(132, [S])
        ident = at(136, [128])
        ones = at(136.5, [128])
        vec = at(137, [128])
        identr = at(137.5, [128], F32R)
        maskr = at(138, [128], F32R)
        invc = at(138.5, [8])
        sd = at(138.53125, [8])
        var = at(138.65625, [8])
        EDGE = at(138.59375, [16])
        WORK = 139

        s_const = sem("s_const")
        t_const = sp.dma(ident[:, :], A["ident"], s_const)
        t_const = sp.dma(vec[:, 0:A["vec"].shape[1]], A["vec"], s_const)
        t_ones = pool.do(lambda e: e.memset(ones[:, :], 1.0))


        def mult(dst, a, b, *after, q=dve):
            return q.do(lambda e: e.tensor_tensor(dst, a, b, ALU.mult), *after)

        def split(src, hi, lo, *after, q=act):
            t = q.do(lambda e: e.activation(hi, src, ACT.Copy), *after) if q is act else \
                q.do(lambda e: e.tensor_scalar(hi, src, 1.0, 0.0, op0=ALU.mult, op1=ALU.add), *after)
            u = dve.do(lambda e: e.tensor_tensor(lo, src, hi.bitcast(F32), ALU.subtract), t, *after)
            return t, u

        def product(ps, terms, *after, begin=True, finish_=True):
            last = len(terms) - 1
            for k, (wh, wl, ah, al, th, tl) in enumerate(terms):
                for i, (l, r) in enumerate(((wh, ah), (wl, ah), (wh, al))):
                    for n in range(2):
                        end = k == last and i == 2
                        first = k == 0 and i == 0 and begin
                        t = pe.do(
                            lambda e, l=l, r=r, n=n, first=first, end=end and finish_:
                            e.matmul(ps[:, 512 * n:512 * n + 512], l, r[:, 512 * n:512 * n + 512],
                                     start=first, stop=end),
                            *(after + tuple(th) if i == 0 else tuple(tl)), mark=end and n == 1)
            return t

        def finish():
            s_out = sem("s_out")
            for m in range(KT):
                t = sp.dma(out[128 * m:128 * m + 128, :], H[:, m, :], s_out, t_h[m])
            sp.wait(t)


        class Weights:
            def __init__(self):
                self.plan, self.loaded, self.used, self.hi, self.lo, self.use = [], [], 0, [], [], []
                self.sems = [sem(f"s_stage{i}") for i in range(3)]

            def add(self, name, tiles):
                self.plan += [A[name][i] for i in tiles]

            def load(self):
                n = len(self.loaded)
                if n < len(self.plan):
                    freed = (self.hi[n - 3], self.lo[n - 3]) if n >= 3 else ()
                    self.loaded.append(sp.dma(STG[n % 3][:, :], self.plan[n], self.sems[n % 3], *freed))

            def split(self):
                n = len(self.hi)
                if n < len(self.plan):
                    freed = (self.use[n - 3],) if n >= 3 else ()
                    t, u = split(STG[n % 3][:, :], WH[n % 3][:, :], WL[n % 3][:, :],
                                 self.loaded[n], *freed)
                    self.hi.append(t)
                    self.lo.append(u)
                    self.load()

            def get(self):
                n = self.used
                self.used += 1
                return WH[n % 3], WL[n % 3], [self.hi[n]], [self.lo[n]]

            def done(self, t):
                self.use.append(t)
                self.split()

        W = Weights()
        W.add("pool_in", [0])
        for g in range(4):
            W.add("pool_in", [4 * g + 1, 4 * g + 2, 4 * g + 3, 16 + 4 * g, 17 + 4 * g])
            W.add("pool_g", [2 * g])
            W.add("pool_in", [18 + 4 * g])
            W.add("pool_out", [4 * g, 4 * g + 1])
            W.add("pool_in", [19 + 4 * g])
            W.add("pool_g", [2 * g + 1])
            if g < 3:
                W.add("pool_in", [4 * g + 4])
            W.add("pool_out", [4 * g + 2, 4 * g + 3])

        for i in range(8):
            W.add("sb_in", [i, 8 + i])
        W.add("sb_v", range(16))
        W.add("sb_in", range(32, 48))
        W.add("sb_out", range(16))
        W.add("gdn_in", [8 + i for i in range(8)] + [i for i in range(8)] + list(range(16, 32)))
        for _ in range(2):
            W.add("gdn_out", range(8))
        W.add("w1", range(4))
        for g in range(8):
            if g < 7:
                W.add("w1", [4 * g + 4])
            W.add("w2", range(4 * g, 4 * g + 4))
            if g < 7:
                W.add("w1", [4 * g + 5, 4 * g + 6, 4 * g + 7])

        P = [at(WORK + 8 * i, [2, S]) for i in range(4)]
        PH = [at(WORK + 8 * i, [S], F32R) for i in range(4)]
        PL = [at(WORK + 8 * i + 4, [S], F32R) for i in range(4)]
        YH = [at(WORK + 32 + 8 * i, [S], F32R) for i in range(2)]
        YL = [at(WORK + 32 + 8 * i + 4, [S], F32R) for i in range(2)]
        XP = at(WORK + 48, [1040])
        tmps = [at(WORK + 52.0625 + 4.0625 * i, [1040]) for i in range(4)]
        TMP = Slots(tmps)

        s_x = [sem(f"s_x{k}") for k in range(KT)]
        t_h = []
        for k in range(KT):
            t_h.append(sp.dma(H[:, k, :], A["xT"][128 * k:128 * k + 128, :], s_x[k]))
            if k == 0:
                W.load()
        W.load()
        W.load()

        class Squares:

            def __init__(self):
                self.acc = None

            def feed(self, x, *after, scale=1.0):
                sq, free = TMP.take()
                t = act.do(lambda e: e.activation(sq[:, 0:S], x, ACT.Square, scale=scale), *after, *free)
                if self.acc is None:
                    self.acc, self.t = sq, t
                else:
                    self.t = pool.do(lambda e: e.tensor_tensor(
                        self.acc[:, 0:S], self.acc[:, 0:S], sq[:, 0:S], ALU.add), t, self.t)
                    TMP.put(sq, self.t)

            def columns(self, ps, free):
                for j in range(8):
                    t = pe.do(lambda e: e.matmul(
                        ps[:, j:j + 1], self.acc[:, 128 * j:128 * j + 128], ones[:, 0:1],
                        start=True, stop=True), self.t, t_ones, *free, mark=j == 7)
                TMP.put(self.acc, t)
                return t

        def inv_sqrt(dst, var, sd, *after):
            t_sd = act.do(lambda e: e.activation(sd, var, ACT.Sqrt), *after)
            t = dve.do(lambda e: e.reciprocal(sd, sd), t_sd)
            t = mult(var, var, sd, t)
            t = mult(var, var, sd, t)
            t = dve.do(lambda e: e.tensor_scalar(var, var, -0.5, 1.5, op0=ALU.mult, op1=ALU.add), t)
            return mult(dst, var, sd, t)

        def spread(col, dst, *after, free=()):
            dg, f = TMP.take()
            for j in range(8):
                t = dve.do(lambda e: e.tensor_scalar(
                    dg[:, 128 * j:128 * j + 128], ident[:, :], col[:, j:j + 1], None,
                    op0=ALU.mult), *after, t_const, *f)
            ps, f = PSW.take()
            for n in range(2):
                t = pe.do(lambda e: e.matmul(
                    ps[:, 512 * n:512 * n + 512], ones[:, :], dg[:, 512 * n:512 * n + 512],
                    start=True, stop=True), t, t_ones, *f, mark=n == 1)
            TMP.put(dg, t)
            t = act.do(lambda e: e.activation(dst, ps[:, :], ACT.Copy), t, *free)
            PSW.put(ps, t)
            return t

        def mean_eps(dst, ps, *after):
            return dve.do(lambda e: e.tensor_scalar(dst, ps, 1.0 / D, EPS, op0=ALU.mult, op1=ALU.add),
                          *after)

        class Norm:

            def __init__(self, gains):
                self.gains = gains
                self.uh, self.ul = [None] * KT, [None] * KT
                self.sq = Squares()

            def feed(self, k, t_h, *free):
                g = self.gains[:, k:k + 1]
                th = act.do(lambda e: e.activation(UH[:, k, :], H[:, k, :], ACT.Copy, scale=g),
                            t_h, t_const, *free)
                tl = dve.do(lambda e: e.scalar_tensor_tensor(
                    UL[:, k, :], H[:, k, :], g, UH[:, k, :].bitcast(F32),
                    op0=ALU.mult, op1=ALU.subtract), th, *free)
                self.uh[k], self.ul[k] = [th], [tl]
                self.sq.feed(H[:, k, :], t_h)

            def finish(self, inv_free=()):
                ps, free = PSW.take()
                t = mean_eps(var[:, :], ps[:, 0:8], self.sq.columns(ps, free))
                PSW.put(ps, t)
                self.t_ic = inv_sqrt(invc[:, :], var[:, :], sd[:, :], t)
                self.t_inv = spread(invc, INV[:, :], self.t_ic, free=inv_free)

        N0 = Norm(vec[:, 0:8])
        for k in range(KT):
            N0.feed(k, t_h[k])
            if k < 3:
                W.split()

        def dense(norm):
            wh, wl, th, tl = W.get()
            ps, free = PSW.take()
            t = product(ps, [(wh[:, 128 * k:128 * k + 128], wl[:, 128 * k:128 * k + 128],
                              UH[:, k, :], UL[:, k, :], th + norm.uh[k] + free, tl + norm.ul[k])
                             for k in range(KT)])
            return ps, t

        memo = {"c": [], "xp": [dve.do(lambda e: e.memset(XP[:, 0:16], 0.0))]}
        t_P = [None] * 4
        t_Pfree = [[] for _ in range(4)]

        def pooled(g, i, ps, t):
            w = 2 << g
            t = dve.do(lambda e: e.tensor_tensor(XP[:, 16:1040], ps[:, :], INV[:, :], ALU.mult),
                       t, N0.t_inv, *memo["xp"])
            PSW.put(ps, t)
            src, d = XP, 1
            bufs = []
            while d < w:
                dst, free = TMP.take()
                lo = 2 * d - 1
                t = dve.do(lambda e, dst=dst, src=src, lo=lo, d=d: e.tensor_tensor(
                    dst[:, lo:1040], src[:, lo:1040], src[:, lo - d:1040 - d], ALU.add), t, *free)
                if src is not XP:
                    TMP.put(src, t)
                src, d = dst, 2 * d
            pf, free = TMP.take()
            t1 = dve.do(lambda e: e.scalar_tensor_tensor(
                pf[:, 16:1040], src[:, 16:1040], 1.0 / w, XP[:, 16:1040],
                op0=ALU.mult, op1=ALU.subtract), t, *free)
            t2 = dve.do(lambda e: e.tensor_tensor(EDGE[:, 0:w], src[:, 16:16 + w], vec[:, VC:VC + w],
                                                  ALU.mult), t, t_const, *memo['c'])
            t = dve.do(lambda e: e.tensor_tensor(pf[:, 16:16 + w - 1], EDGE[:, 0:w - 1],
                                                 XP[:, 16:16 + w - 1], ALU.subtract), t1, t2)
            memo["xp"] = memo["c"] = [t]
            TMP.put(src, t)
            th, tl = split(pf[:, 16:1040], PH[i][:, :], PL[i][:, :], t, *t_Pfree[i])
            TMP.put(pf, th, tl)
            t_P[i] = (th, tl)

        VC = 8
        Yslots = Slots([0, 1])
        ys = []

        def x_tile(g, i):
            ps, t = dense(N0)
            pooled(g, i, ps, t)
            W.done(t)

        def z_tile(g, i):
            ps, t = dense(N0)
            z, free = TMP.take()
            tz = mult(z[:, 0:S], ps[:, :], INV[:, :], t, N0.t_inv, *free)
            PSW.put(ps, tz)
            tz = act.do(lambda e: e.activation(z[:, 0:S], z[:, 0:S], ACT.Silu), tz)
            W.done(t)
            return z, tz

        def g_tile(g, i, z, tz, w):
            wh, wl, th, tl = w
            ps, free = PSW.take()
            o = 512 * (i % 2)
            t = product(ps, [(wh[:, o + 128 * k:o + 128 * k + 128], wl[:, o + 128 * k:o + 128 * k + 128],
                              PH[k][:, :], PL[k][:, :], th + [t_P[k][0]] + free, tl + [t_P[k][1]])
                             for k in range(4)])
            y, free = TMP.take()
            sc = vec[:, VS + 4 * g + i:VS + 4 * g + i + 1]
            ty = dve.do(lambda e: e.scalar_tensor_tensor(y[:, 0:S], ps[:, :], sc, z[:, 0:S],
                                                         op0=ALU.mult, op1=ALU.mult), t, tz, t_const, *free)
            PSW.put(ps, ty)
            TMP.put(z, ty)
            b, free = Yslots.take()
            t1, t2 = split(y[:, 0:S], YH[b][:, :], YL[b][:, :], ty, *free)
            TMP.put(y, t1, t2)
            ys.append((b, [t1], [t2]))
            return t

        VS = 24

        def out_tiles(parts, m0, m1, last=None):
            n = len(parts)
            wh, wl, th, tl = W.get()
            for m in range(m0, m1):
                ps, free = PSW.take()
                o = 128 * n * (m - m0)
                t = product(ps, [(wh[:, o + 128 * k:o + 128 * k + 128], wl[:, o + 128 * k:o + 128 * k + 128],
                                  ah, al, th + ta + free, tl + tb)
                                 for k, (ah, al, ta, tb) in enumerate(parts)])
                t_h[m] = dve.do(lambda e, m=m, ps=ps: e.tensor_tensor(
                    H[:, m, :], H[:, m, :], ps[:, :], ALU.add), t, t_h[m])
                PSW.put(ps, t_h[m])
                if last:
                    last(m)
            W.done(t)
            return t

        def pool_out(last=None):
            parts = [(YH[b][:, :], YL[b][:, :], a, c) for b, a, c in ys]
            out_tiles(parts, 0, 4, last)
            t = out_tiles(parts, 4, 8, last)
            for b, _, _ in ys:
                Yslots.put(b, t)
            ys.clear()

        x_tile_first = dense(N0)
        N0.finish()
        pooled(0, 0, *x_tile_first)
        W.done(x_tile_first[1])
        for g in range(4):
            for i in range(1, 4):
                x_tile(g, i)
            for pair in range(2):
                za = z_tile(g, 2 * pair)
                if pair:
                    pool_out()
                zb = z_tile(g, 2 * pair + 1)
                t_u = W.use[-1]
                t_inv_old = zb[1]
                w = W.get()
                g_tile(g, 2 * pair, *za, w)
                t = g_tile(g, 2 * pair + 1, *zb, w)
                if pair:
                    for i in range(4):
                        t_Pfree[i] = [t]
                W.done(t)
            if g < 3:
                x_tile(g + 1, 0)
                pool_out()
            else:
                N1 = Norm(vec[:, 40:48])
                if upto > 1:
                    pool_out(lambda m: N1.feed(m, t_h[m], t_u))
                else:
                    pool_out()

        if upto == 1:
            return finish()
        QKD = nc.dram_tensor("qk_split", [2, 2, 1024, S], F32).ap()
        VD = nc.dram_tensor("v_split", [2, 16, 128, 8, 128], F32).ap()
        ZD = nc.dram_tensor("z_gate", [16, 128, S], F32).ap()
        QS = Slots([(at(WORK + 8 * i, [S], F32R), at(WORK + 8 * i + 4, [S], F32R),
                     sem(f"s_qs{i}"), sem(f"s_ql{i}")) for i in range(2)], t_Pfree[0])
        VS_ = Slots([(at(WORK + 16 + 4 * i, [512], F32R), at(WORK + 18 + 4 * i, [512], F32R),
                      sem(f"s_vs{i}"), sem(f"s_vl{i}")) for i in range(4)], t_Pfree[0])
        s_zd = [sem(f"s_zd{i}") for i in range(4)]
        t_qk, t_v, t_z = {}, {}, {}

        def qk_tile(kind, i, ps, t):
            f, free = TMP.take()
            if kind == 0:
                te = dve.do(lambda e: e.scalar_tensor_tensor(
                    f[:, 0:S], ps[:, :], 0.125, INV[:, :], op0=ALU.mult, op1=ALU.mult), t, N.t_inv, *free)
            else:
                te = mult(f[:, 0:S], ps[:, :], INV[:, :], t, N.t_inv, *free)
            PSW.put(ps, te)
            slot, free = QS.take()
            hi, lo, sh, sl = slot
            th, tl = split(f[:, 0:S], hi[:, :], lo[:, :], te, *free)
            TMP.put(f, th, tl)
            a = sp.dma(QKD[kind, 0, 128 * i:128 * i + 128, :], hi[:, :], sh, th)
            b = sp.dma(QKD[kind, 1, 128 * i:128 * i + 128, :], lo[:, :], sl, tl)
            QS.put(slot, a, b)
            t_qk[kind, i] = (a, b)

        N = N1
        first = [W.get(), W.get()]
        fps = [PSW.take(), PSW.take()]
        ft = [None, None]
        for part in ((0, 6), (6, 8)):
            for x in range(2):
                wh, wl, th, tl = first[x]
                ps, free = fps[x]
                ft[x] = product(ps, [(wh[:, 128 * k:128 * k + 128], wl[:, 128 * k:128 * k + 128],
                                      UH[:, k, :], UL[:, k, :], th + N.uh[k] + free, tl + N.ul[k])
                                     for k in range(*part)], begin=part[0] == 0, finish_=part[1] == 8)
        N.finish([t_inv_old])
        for x in range(2):
            qk_tile(x, 0, fps[x][0], ft[x])
            W.done(ft[x])
        for i in range(2, 16):
            ps, t = dense(N)
            qk_tile(i % 2, i // 2, ps, t)
            W.done(t)

        for g in range(4):
            pss = [PSW.take() for _ in range(4)]
            for k in range(8):
                if k % 2 == 0:
                    wh, wl, th, tl = W.get()
                r = slice(512 * (k % 2), 512 * (k % 2) + 512)
                ends = []
                for j in range(8):
                    ps, free = pss[j // 2]
                    o = slice(512 * (j % 2), 512 * (j % 2) + 512)
                    js = slice(128 * j, 128 * j + 128)
                    for i, (l, m) in enumerate(((UH, wh), (UL, wh), (UH, wl))):
                        t = pe.do(lambda e, ps=ps, o=o, l=l, m=m, js=js, k=k, r=r, i=i: e.matmul(
                            ps[:, o], l[:, k, js], m[:, r], start=k == 0 and i == 0,
                            stop=k == 7 and i == 2), *(th + free + N.uh[k] if i == 0 else tl + N.ul[k]),
                            mark=i == 2 and (k == 7 or j == 7))
                    ends.append(t)
                if k % 2 == 1 and k < 7:
                    W.done(t)
            for j in range(8):
                ps = pss[j // 2][0]
                o = slice(512 * (j % 2), 512 * (j % 2) + 512)
                slot, free = VS_.take()
                hi, lo, sh, sl = slot
                th = act.do(lambda e, ps=ps, o=o, j=j, hi=hi: e.activation(
                    hi[:, :], ps[:, o], ACT.Copy, scale=invc[:, j:j + 1]), ends[j], N.t_ic, *free)
                tl = dve.do(lambda e, ps=ps, o=o, j=j, hi=hi, lo=lo: e.scalar_tensor_tensor(
                    lo[:, :], ps[:, o], invc[:, j:j + 1], hi[:, :].bitcast(F32),
                    op0=ALU.mult, op1=ALU.subtract), th, *free)
                if j % 2:
                    PSW.put(ps, th, tl)
                hs = slice(4 * g, 4 * g + 4)
                a = sp.dma(VD[0, hs, :, j, :].rearrange("h p c -> p h c"),
                           hi[:, :].rearrange("p (h c) -> p h c", h=4), sh, th)
                b = sp.dma(VD[1, hs, :, j, :].rearrange("h p c -> p h c"),
                           lo[:, :].rearrange("p (h c) -> p h c", h=4), sl, tl)
                VS_.put(slot, a, b)
                t_v[g, j] = (a, b)
            W.done(t)

        def gate(i, ps, t):
            z, free = TMP.take()
            tz = mult(z[:, 0:S], ps[:, :], INV[:, :], t, N.t_inv, *free)
            PSW.put(ps, tz)
            tz = act.do(lambda e: e.activation(z[:, 0:S], z[:, 0:S], ACT.Silu), tz)
            W.done(t)
            t_z[i] = sp.dma(ZD[i], z[:, 0:S], s_zd[tmps.index(z)], tz)
            TMP.put(z, t_z[i])
            t_gates.extend((t_z[i], tz))

        t_gates = []
        NZ = 14
        t_idr = pool.do(lambda e: e.tensor_copy(identr[:, :], ident[:, :]), t_const)
        s_mask = sem("s_mask")
        mk, f = TMP.take()
        t_mask = sp.dma(mk[:, 0:128], A["mask"], s_mask, *f)
        t_mask = pool.do(lambda e: e.tensor_copy(maskr[:, :], mk[:, 0:128]), t_mask)
        TMP.put(mk, t_mask)

        for i in range(NZ):
            gate(i, *dense(N))

        keep = []
        for _ in range(4):
            t, f = TMP.take()
            if t in tmps[:2]:
                keep += f
            else:
                TMP.put(t, *f)
        q_free = keep + [tok for ring in (QS, VS_) for _, f in ring.line for tok in f]
        t_u1 = []

        def slot_head(i, kb, free):
            HEADS.line.append((dict(
                kx=at(kb, [S], F32R), q1=at(kb + 4, [S], F32R), q2=at(kb + 8, [S], F32R),
                vh=at(kb + 12, [8, 128], F32R), vl=at(kb + 16, [8, 128], F32R), z=at(kb + 20, [S]),
                s=[sem(f"s_head{i}_{j}") for j in range(4)]), free))

        HEADS = Slots([])
        slot_head(0, 139, q_free)
        slot_head(1, 32, t_u1)

        def load_head(h):
            b, free = HEADS.take()
            p = h // 2
            r = slice(64 * h, 64 * h + 64)
            for j, (kind, hi, lo) in enumerate((("kx", 0, 1), ("q1", 0, 0), ("q2", 1, 1))):
                kq = 1 if j == 0 else 0
                sp.dma(b[kind][0:64, :], QKD[kq, hi, r, :], b["s"][j], *free, t_qk[kq, p][hi])
                b["t" + kind] = sp.dma(b[kind][64:128, :], QKD[kq, lo, r, :], b["s"][j],
                                       *free, t_qk[kq, p][lo])
            toks = [tok for j in range(8) for tok in t_v[h // 4, j]]
            sp.dma(b["vh"][:, :, :], VD[0, h], b["s"][3], *free, *toks)
            sp.dma(b["vl"][:, :, :], VD[1, h], b["s"][3], *free, *toks)
            b["tv"] = sp.dma(b["z"][:, :], ZD[h], b["s"][3], *free, t_z[h])
            return b

        banks = [PSW.take() for _ in range(3)]
        half = [((b, n), f) for b, f in banks for n in range(2)]

        def bank(b):
            return b[0][:, 512 * b[1]:512 * b[1] + 512]

        LG, TP, OA = Slots([]), Slots([]), Slots([])
        for i, (b, f) in enumerate(half):
            (LG if i < 3 else TP if i < 5 else OA).put(b, *f)
        def ring(kbs, make):
            r = Slots([])
            for kb in kbs:
                r.line.append((make(kb), t_u1 if kb < 100 else q_free))
            return r

        OMB = ring((163, 171, 179, 187), lambda kb: (at(kb, [S]), at(kb + 4, [S])))
        ATS = ring((56, 60, 84, 88, 92), lambda kb: (at(kb, [512], F32R), at(kb + 2, [512], F32R)))
        YF = ring((64,), lambda kb: at(kb, [S]))
        YS = ring((68, 76), lambda kb: (at(kb, [S], F32R), at(kb + 4, [S], F32R)))
        YS.line.append(((at(195, [S], F32R), at(132, [S], F32R)), t_gates))
        YS.line.append(((at(199.1875, [S], F32R), at(203.1875, [S], F32R)), t_gates))

        heads = {}

        def logits(h, tt):
            b = heads[h]
            n = 128 * (tt + 1)
            om_bt, free = OMB.take()
            om, bt = om_bt
            qs = slice(128 * tt, 128 * tt + 128)
            t_sig = []
            res = {}

            def unit(c0):
                c1 = min(c0 + 512, n)
                lg, f = LG.take()
                ps = bank(lg)
                diag = c1 == n
                pe.do(lambda e: e.matmul(ps[:, 0:c1 - c0], b["q1"][:, qs], b["kx"][:, c0:c1],
                                         start=True, stop=False), b["tkx"], b["tq1"], *f, mark=False)
                t = pe.do(lambda e: e.matmul(ps[:, 0:c1 - c0], b["q2"][:, qs], b["kx"][:, c0:c1],
                                             start=False, stop=not diag), b["tq2"], mark=not diag)
                if diag:
                    t = pe.do(lambda e: e.matmul(ps[:, c1 - c0 - 128:c1 - c0], identr[:, :],
                                                 maskr[:, :], start=False, stop=True), t_idr, t_mask)
                t1 = act.do(lambda e: e.activation(om[:, c0:c1], ps[:, 0:c1 - c0], ACT.Sigmoid,
                                                   scale=-1.0), t, *free)
                t2 = act.do(lambda e: e.activation(bt[:, c0:c1], ps[:, 0:c1 - c0], ACT.Sigmoid), t, *free)
                LG.put(lg, t1, t2)
                t_sig.extend((t1, t2))
                if diag:
                    rev = om[:, n - 1::-1]
                    ts = dve.do(lambda e: e.tensor_tensor_scan(rev, rev, rev, 1.0, ALU.mult, ALU.bypass),
                                *t_sig)
                    res["A"] = pool.do(lambda e: e.tensor_tensor(
                        bt[:, 0:n - 1], bt[:, 0:n - 1], om[:, 1:n], ALU.mult), ts, *t_sig)

            for c0 in range(0, n, 512):
                yield (lambda c0=c0: unit(c0)), (min(n - c0, 512) * 2 + 128) / 2400
            tiles_A[h, tt] = (om_bt, bt, res)

        tiles_A = {}

        def weigh(h, p):
            b = heads[h]
            st = {}

            def turn(m):
                tp, f = TP.take()
                ps = bank(tp)
                if m == 0:
                    st["a"] = [tiles_A[h, 2 * p + i] for i in range(2)]
                blocks = [(0, 2 * m, 0), (1, 2 * m, 128)]
                blocks += [(1, 2 * m + 1, 256)] if m == p else [(0, 2 * m + 1, 256), (1, 2 * m + 1, 384)]
                for x, j, o in blocks:
                    _, bt, res = st["a"][x]
                    t = pe.do(lambda e, bt=bt, j=j, o=o: e.transpose(
                        ps[:, o:o + 128], bt[:, 128 * j:128 * j + 128], ident[:, :]), res["A"], *f,
                        mark=o == blocks[-1][2])
                n = 128 * len(blocks)
                if m == p:
                    for x in range(2):
                        OMB.put(st["a"][x][0], t)
                at_, f = ATS.take()
                hi, lo = at_
                th = act.do(lambda e: e.activation(hi[:, 0:n], ps[:, 0:n], ACT.Copy), t, *f)
                tl = dve.do(lambda e: e.tensor_tensor(lo[:, 0:n], ps[:, 0:n], hi[:, 0:n].bitcast(F32),
                                                      ALU.subtract), th, *f)
                TP.put(tp, tl)
                st[m] = (at_, th, tl)

            def times(m):
                if m == 0:
                    st["o"], st["of"] = OA.take()
                ps = bank(st["o"])
                (hi, lo), th, tl = st[m][0], st[m][1], st[m][2]
                for i in range(2):
                    j = 2 * m + i
                    c = slice(128, 256) if m == p and i else slice(0, 256)
                    src = slice(256, 384) if m == p and i else slice(256 * i, 256 * i + 256)
                    for x, (v, a) in enumerate((("vh", hi), ("vl", hi), ("vh", lo))):
                        end = m == p and i == 1 and x == 2
                        t = pe.do(lambda e, v=v, a=a, j=j, c=c, src=src, s=m == 0 and i == 0 and x == 0,
                                  end=end: e.matmul(ps[:, c], b[v][:, j, :], a[:, src], start=s, stop=end),
                                  b["tv"], *(st["of"] if m == 0 else []), th if x < 2 else tl,
                                  mark=i == 1 and x == 2)
                ATS.put(st[m][0], t)
                if m == p:
                    if p == 0:
                        st["yf"] = yf_now[h] = YF.take()
                    yf, f = yf_now[h]
                    c = slice(256 * p, 256 * p + 256)
                    ty = dve.do(lambda e: e.tensor_tensor(yf[:, c], ps[:, 0:256], b["z"][:, c], ALU.mult),
                                t, b["tv"], *f)
                    OA.put(st["o"], ty)
                    if p == 3:
                        y, f = YS.take()
                        t1, t2 = split(yf[:, :], y[0][:, :], y[1][:, :], ty, *f)
                        YF.put(yf, t1, t2)
                        HEADS.put(b, t, ty)
                        y_now.append((y, [t1], [t2]))

            lag = 1
            for m in range(p + 1 + lag):
                if m <= p:
                    yield (lambda m=m: turn(m)), 4 * 110 / 2000
                if m >= lag:
                    yield (lambda m=m - lag: times(m)), 6 * 256 / 2400

        yf_now, y_now = {}, []

        filler = []

        def z_parts(i):
            box = {}

            def part(c):
                if c == 0:
                    box["w"], box["ps"] = W.get(), PSW.take()
                wh, wl, th, tl = box["w"]
                ps, free = box["ps"]
                t = product(ps, [(wh[:, 128 * k:128 * k + 128], wl[:, 128 * k:128 * k + 128],
                                  UH[:, k, :], UL[:, k, :], th + free, tl)
                                 for k in (2 * c, 2 * c + 1)], begin=c == 0, finish_=c == 3)
                if c == 3:
                    gate(i, ps, t)
                    if i == 15:
                        t_u1.append(t)
                        take_wbanks()
            return [lambda c=c: part(c) for c in range(4)]

        WB = Slots([])

        def take_wbanks():
            b, f = PSW.take()
            for n in range(2):
                WB.put((b, n), *f)

        def out_half(parts, m, n, first, last, t_hold, m0):
            if first:
                w_now[0] = W.get()
            wh, wl, th, tl = w_now[0]
            wb, f = WB.take()
            ps = bank(wb)
            c = slice(512 * n, 512 * n + 512)
            for k, (ah, al, ta, tb) in enumerate(parts):
                o = 256 * (m - m0) + 128 * k
                for i, (l, r) in enumerate(((wh, ah), (wl, ah), (wh, al))):
                    end = k == 1 and i == 2
                    t = pe.do(lambda e, l=l, r=r, o=o, s=k == 0 and i == 0, end=end: e.matmul(
                        ps[:, :], l[:, o:o + 128], r[:, c], start=s, stop=end),
                        *(th + ta + f if i == 0 else tl + tb), mark=end)
            t_h[m] = dve.do(lambda e: e.tensor_tensor(H[:, m, c], H[:, m, c], ps[:, :], ALU.add),
                            t, t_h[m])
            WB.put(wb, t_h[m])
            if last:
                W.done(t)
            t_hold[0] = t

        w_now = [None]

        def out_atoms(hook=None):
            pair = y_now[:2]
            del y_now[:2]
            parts = [(y[0], y[1], a, c) for y, a, c in pair]
            hold = [None]
            atoms = []
            for m in range(8):
                for n in range(2):
                    def atom(m=m, n=n):
                        out_half(parts, m, n, m % 4 == 0 and n == 0, m % 4 == 3 and n == 1, hold, m // 4 * 4)
                        if m == 7 and n == 1:
                            for y, _, _ in pair:
                                YS.put(y, hold[0])
                        if hook and n == 1:
                            hook(m)
                    atoms.append(atom)
            return atoms

        heads[0] = load_head(0)
        steps = [(h, p) for h in range(16) for p in range(4)]

        def pair_logits(h, p):
            return [fn for tt in (2 * p, 2 * p + 1) for fn, _ in logits(h, tt)]

        for i in (14, 15):
            for fn in pair_logits(0, i - 14) + z_parts(i):
                fn()
        FILL = (3, 2, 1, 2)
        for P, (h, p) in enumerate(steps):
            todo = []
            if p == 0 and h < 15:
                heads[h + 1] = load_head(h + 1)
            if 1 <= P < len(steps) - 1:
                q = pair_logits(*steps[P + 1])
                todo += [(0.6 * i / len(q), 0, fn) for i, fn in enumerate(q)]
            ta = list(weigh(h, p))
            todo += [((i + 0.3) / len(ta), 1, fn) for i, (fn, _) in enumerate(ta)]
            nf = FILL[p]
            fl, filler = filler[:nf], filler[nf:]
            todo += [((i + 0.5) / len(fl), 2, fn) for i, fn in enumerate(fl)]
            for _, _, fn in sorted(todo, key=lambda x: x[:2]):
                fn()
            if p == 3 and h % 2 and h < 15:
                filler += out_atoms()
        for fn in filler:
            fn()

        end = [(q.sem, q.count) for q in (pe, act, dve, pool)]
        PSW = Slots([])
        for ps in psum:
            PSW.put(ps, *[tok for ring in (LG, TP, OA, WB) for (b, _), f in ring.line if b is ps for tok in f])
        TMP = Slots([])
        tmps = [at(149.3125 + 4 * i, [S]) for i in range(7)]
        for t in tmps:
            TMP.put(t, *end)
        small = iter([at(141.5 + 0.25 * i, [64]) for i in range(15)])
        TI, TS = at(139, [128]), at(139.5, [128])
        wab_h, wab_l = at(140, [128], F32R), at(140.5, [128], F32R)
        gfm = at(141, [8])
        cg = at(141.0625, [112])
        CB = at(145.25, [1040])

        s_g = sem("s_g")
        sp.dma(TI[:, :], A["tri_incl"], s_g, *end)
        sp.dma(TS[:, :], A["tri_strict"], s_g, *end)
        t_cg = sp.dma(cg[:, :], A["gdn_vec"], s_g, *end)
        t_gfm = mult(gfm[:, :], vec[:, 48:56], vec[:, 56:64], t_const, *end)
        t_pad = dve.do(lambda e: e.memset(CB[:, 0:16], 0.0), *end)

        parts = [(y[0], y[1], a, c) for y, a, c in y_now]
        N2 = Norm(gfm)
        sq_f = Squares()

        def feed2(m):
            N2.feed(m, t_h[m], t_gfm, *end)
            sq_f.feed(H[:, m, :], t_h[m], scale=vec[:, 48 + m:49 + m])

        out_tiles(parts, 0, 4, feed2)
        t = out_tiles(parts, 4, 8, feed2)
        if upto == 2:
            return finish()
        t_last = [t]

        def dense_pair(norm):
            w = [W.get(), W.get()]
            ps = [PSW.take(), PSW.take()]
            res = [None, None]
            for part in ((0, 6), (6, 8)):
                for x in range(2):
                    wh, wl, th, tl = w[x]
                    res[x] = product(ps[x][0], [
                        (wh[:, 128 * k:128 * k + 128], wl[:, 128 * k:128 * k + 128],
                         UH[:, k, :], UL[:, k, :], th + norm.uh[k] + ps[x][1], tl + norm.ul[k])
                        for k in range(*part)], begin=part[0] == 0, finish_=part[1] == 8)
            return [(ps[x][0], res[x]) for x in range(2)]

        pair = dense_pair(N2)
        W.done(pair[0][1])
        W.done(pair[1][1])

        s_ab = sem("s_ab")
        ab, f = TMP.take()
        t = sp.dma(ab[:, 0:128], A["gdn_ab"], s_ab, *f)
        t1, t2 = split(ab[:, 0:128], wab_h[:, :], wab_l[:, :], t)
        TMP.put(ab, t1, t2)
        psab, f = PSW.take()
        for k in range(8):
            for i, (l, r) in enumerate(((wab_h, UH), (wab_l, UH), (wab_h, UL))):
                for n in range(2):
                    t_ab = pe.do(lambda e: e.matmul(
                        psab[0:16, 512 * n:512 * n + 512], l[:, 16 * k:16 * k + 16],
                        r[:, k, 512 * n:512 * n + 512], start=k == 0 and i == 0,
                        stop=k == 7 and i == 2), t1, t2, *f, mark=k == 7 and i == 2)

        ps, f = PSW.take()
        ivf, var2 = next(small), next(small)
        t = N2.sq.columns(ps, f)
        t2 = sq_f.columns(ps[:, 8:16], f)
        t = mean_eps(var[:, :], ps[:, 0:8], t, t2)
        tb = dve.do(lambda e: e.tensor_scalar(var2[:, 0:8], ps[:, 8:16], 1.0 / D, None, op0=ALU.mult),
                    t2, *end)
        PSW.put(ps, tb, t)
        t_f = inv_sqrt(ivf[:, 0:8], var[:, :], sd[:, :], t, *end)
        t = mult(var2[:, 0:8], var2[:, 0:8], ivf[:, 0:8], tb, t_f)
        t = mult(var2[:, 0:8], var2[:, 0:8], ivf[:, 0:8], t)
        t = dve.do(lambda e: e.tensor_scalar(var2[:, 0:8], var2[:, 0:8], EPS, None, op0=ALU.add), t)
        t = inv_sqrt(invc[:, :], var2[:, 0:8], sd[:, :], t)
        t = mult(invc[:, :], invc[:, :], ivf[:, 0:8], t)
        N2.t_inv = spread(invc, INV[:, :], t, free=t_last)
        IV1, f1 = TMP.take()
        t = spread(ivf, IV1[:, :], t_f, free=f1)
        t_x2 = []
        for m in range(KT):
            g = vec[:, 48 + m:49 + m]
            t_h[m] = dve.do(lambda e: e.scalar_tensor_tensor(
                H[:, m, :], H[:, m, :], g, IV1[:, :], op0=ALU.mult, op1=ALU.mult),
                t, N2.ul[m][0], sq_f.t)
        TMP.put(IV1, t_h[7])
        if upto == 3:
            return finish()

        HD = nc.dram_tensor("x2", [KT, 128, S], F32).ap()
        KTD, KDD, QTD, QKT, VPD, GTD = (
            nc.dram_tensor(n, [8, 128, 8, 128], F32).ap() for n in ("kt", "kd", "qt", "qkt", "vp", "gt"))
        LTD = nc.dram_tensor("lt", [64, 128, 128], F32).ap()
        UD = nc.dram_tensor("ut", [64, 128, 128], F32).ap()
        TBD = nc.dram_tensor("tb", [128, 32, 32], F32).ap()
        UBD = nc.dram_tensor("ub", [128, 32, 32], F32).ap()
        T64 = nc.dram_tensor("t64", [64, 64, 64], F32).ap()

        s_tmp = {id(t): sem(f"s_gtmp{i}") for i, t in enumerate(tmps)}

        def store(dst, t, *after):
            tok = sp.dma(dst, t[:, :].rearrange("p (b c) -> p b c", b=8), s_tmp[id(t)], *after)
            TMP.put(t, tok, *after)
            return tok

        s_hd = sem("s_hd")
        for m in range(KT):
            t_hd = sp.dma(HD[m], H[:, m, :], s_hd, t_h[m])
        E = [at(4 * h, [8, 128]) for h in range(8)]

        s_zero = sem("s_zero")
        zt, f = TMP.take()
        tz = pool.do(lambda e: e.memset(zt[:, :], 0.0), *f)
        for i in range(8):
            t_zero = sp.dma(UD[8 * i:8 * i + 8].rearrange("n (x y) c -> (n x) (y c)", x=16), zt[:, :],
                            s_zero, tz)
        for i in range(2):
            t_zero = sp.dma(T64[32 * i:32 * i + 32].rearrange("n (x y) c -> (n x) (y c)", x=4),
                            zt[:, :], s_zero, tz)
        TMP.put(zt, t_zero)

        abT, f = TMP.take()
        t = mult(abT[0:16, :], psab[0:16, :], INV[0:16, :], t_ab, N2.t_inv, *f)
        PSW.put(psab, t)
        psa, f = PSW.take()
        for j in range(8):
            t2 = pe.do(lambda e: e.transpose(psa[:, 16 * j:16 * j + 16], abT[0:16, 128 * j:128 * j + 128],
                                             ident[0:16, 0:16]), t, *f, mark=j == 7)
        TMP.put(abT, t2)
        pab = psa[:, 0:128].rearrange("p (b c) -> p b c", b=8)
        gg, spl, beta, eG, eGLG, eGL, ssk, nk, bc, cneg, ssq = (next(small) for _ in range(11))

        def v3(t):
            return t[:, :].rearrange("p (b c) -> p b c", b=8)

        def row(c):
            return cg[:, c:c + 8].unsqueeze(1).broadcast_to([128, 8, 8])

        ta = dve.do(lambda e: e.tensor_tensor(v3(gg), pab[:, :, 0:8], row(104), ALU.add), t2, t_cg, *end)
        tb = dve.do(lambda e: e.tensor_scalar(v3(beta), pab[:, :, 8:16], 1.0, None, op0=ALU.mult), t2, *end)
        PSW.put(psa, ta, tb)
        t_be = act.do(lambda e: e.activation(beta[:, :], beta[:, :], ACT.Sigmoid), tb)
        t1 = act.do(lambda e: e.activation(spl[:, :], gg[:, :], ACT.Abs), ta)
        t1 = act.do(lambda e: e.activation(spl[:, :], spl[:, :], ACT.Exp, scale=-1.0), t1)
        te = act.do(lambda e: e.activation(cneg[:, 0:8], cg[:, 96:104], ACT.Exp), t_cg, *end)
        t2 = dve.do(lambda e: e.tensor_scalar(nk[:, :], spl[:, :], 1.0, None, op0=ALU.add), t1, *end)
        t3 = act.do(lambda e: e.activation(eG[:, :], nk[:, :], ACT.Ln), t2)
        t4 = dve.do(lambda e: e.scalar_tensor_tensor(spl[:, :], nk[:, :], -1.0, spl[:, :],
                                                     op0=ALU.add, op1=ALU.subtract), t2)
        t5 = dve.do(lambda e: e.reciprocal(nk[:, :], nk[:, :]), t4, t3)
        t5 = mult(spl[:, :], spl[:, :], nk[:, :], t5)
        t5 = dve.do(lambda e: e.tensor_tensor(spl[:, :], eG[:, :], spl[:, :], ALU.subtract), t5, t3)
        t5 = dve.do(lambda e: e.scalar_tensor_tensor(spl[:, :], gg[:, :], 0.0, spl[:, :],
                                                     op0=ALU.max, op1=ALU.add), t5)
        t_g = dve.do(lambda e: e.scalar_tensor_tensor(
            v3(gg), v3(spl), -1.0, cneg[:, 0:8].unsqueeze(1).broadcast_to([128, 8, 8]),
            op0=ALU.mult, op1=ALU.mult), t5, te)
        psg, f = PSW.take()
        for i, (l, tl) in enumerate(((TI, t_cg), (TS, t_cg), (ones, t_ones))):
            t = pe.do(lambda e: e.matmul(psg[:, 64 * i:64 * i + 64], l[:, :], gg[:, :],
                                         start=True, stop=True), t_g, tl, *f)
        for i, d in enumerate((eG, eGLG, eGL)):
            t_eg = act.do(lambda e: e.activation(d[:, :], psg[:, 64 * i:64 * i + 64], ACT.Exp), t, t5)
        PSW.put(psg, t_eg)
        eGn = next(small)
        t_egn = dve.do(lambda e: e.tensor_scalar(eGn[:, :], eG[:, :], -1.0, None, op0=ALU.mult),
                       t_eg, *end)
        t_E = []
        for h in range(8):
            gt, f = TMP.take()
            t = dve.do(lambda e: e.tensor_tensor(
                gt[:, :].rearrange("p (b c) -> p b c", b=8),
                TI[:, :].unsqueeze(1).broadcast_to([128, 8, 128]),
                v3(gg)[:, :, h:h + 1].broadcast_to([128, 8, 128]), ALU.mult), t_g, t_cg, *f)
            ps, f = PSW.take()
            for n in range(2):
                t2 = pe.do(lambda e: e.matmul(ps[:, 512 * n:512 * n + 512], TS[:, :],
                                              gt[:, 512 * n:512 * n + 512], start=True, stop=True),
                           t, *f, mark=n == 1)
            TMP.put(gt, t2)
            t_E.append(act.do(lambda e: e.activation(
                E[h][:, :, :].rearrange("p b c -> p (b c)"), ps[:, :], ACT.Exp), t2, t_hd))
            PSW.put(ps, t_E[h])

        cb = {"free": [t_pad]}

        def conv_silu(c, ps, t):
            t = dve.do(lambda e: e.tensor_tensor(CB[:, 16:1040], ps[:, :], INV[:, :], ALU.mult),
                       t, N2.t_inv, *cb["free"])
            PSW.put(ps, t)
            a, f = TMP.take()
            t = act.do(lambda e: e.activation(a[:, :], CB[:, 16:1040], ACT.Copy,
                                              scale=cg[:, 4 * c + 3:4 * c + 4]), t, t_cg, *f)
            for i in (2, 1, 0):
                t = dve.do(lambda e: e.scalar_tensor_tensor(
                    a[:, :], CB[:, 13 + i:1037 + i], cg[:, 4 * c + i:4 * c + i + 1], a[:, :],
                    op0=ALU.mult, op1=ALU.add), t)
            cb["free"] = [t]
            return a, act.do(lambda e: e.activation(a[:, :], a[:, :], ACT.Silu), t)

        def natural(a, t):
            ps, f = PSW.take()
            for j in range(8):
                t2 = pe.do(lambda e: e.transpose(ps[:, 128 * j:128 * j + 128],
                                                 a[:, 128 * j:128 * j + 128], ident[:, :]),
                           t, t_const, *f, mark=j == 7)
            return ps, t2

        def blocks(l, r, *after):
            ps, f = PSW.take()
            for j in range(8):
                t = pe.do(lambda e: e.matmul(ps[:, 128 * j:128 * j + 128], l[:, 128 * j:128 * j + 128],
                                             r[:, 128 * j:128 * j + 128], start=True, stop=True),
                          *after, *f, mark=j == 7)
            return ps, t

        def b3(x):
            return x.rearrange("p (b c) -> p b c", b=8)

        def per_row(col, h):
            return v3(col)[:, :, h:h + 1].broadcast_to([128, 8, 128])

        def square_rows(ps, t, dst, h):
            sq, f = TMP.take()
            t1 = act.do(lambda e: e.activation(sq[:, :], ps[:, :], ACT.Square), t, *f)
            t2 = dve.do(lambda e: e.tensor_reduce(v3(dst)[:, :, h], b3(sq[:, :]), AX.X, ALU.add), t1)
            TMP.put(sq, t2)
            return t1, t2

        t_kt, t_kd, t_lt, t_b = [], [], [], []

        def k_head(h, ps, t):
            a, ta = conv_silu(8 + h, ps, t)
            psn, t = natural(a, ta)
            t_sq, t_ss = square_rows(psn, t, ssk, h)
            kd, f = TMP.take()
            t1 = dve.do(lambda e: e.tensor_tensor(b3(kd[:, :]), b3(psn[:, :]), per_row(eGLG, h),
                                                  ALU.mult), t, t_eg, t_sq, *f)
            PSW.put(psn, t1)
            t_kd.append(store(KDD[:, :, h, :].rearrange("b p c -> p b c"), kd, t1))
            psk, t = blocks(a, a, ta)
            c = [v3(x)[:, :, h] for x in (ssk, bc, cneg, beta)]
            t1 = dve.do(lambda e: e.tensor_scalar(c[0], c[0], EPS, None, op0=ALU.add), t_ss)
            t1 = dve.do(lambda e: e.reciprocal(c[1], c[0]), t1, *end)
            t1 = mult(c[1], c[1], c[3], t1, t_be)
            t_b.append(t1)
            t1 = dve.do(lambda e: e.tensor_scalar(c[2], c[1], -1.0, None, op0=ALU.mult), t1, t_g)
            lt, f = TMP.take()
            t2 = dve.do(lambda e: e.tensor_tensor(b3(lt[:, :]), b3(psk[:, :]), E[h][:, :, :], ALU.mult),
                        t, t_E[h], *f)
            PSW.put(psk, t2)
            t2 = pool.do(lambda e: e.tensor_tensor(b3(lt[:, :]), b3(lt[:, :]), per_row(cneg, h),
                                                   ALU.mult), t2, t1)
            t_lt.append(store(LTD[h::8].rearrange("b p c -> p b c"), lt, t2))
            t_kt.append(store(KTD[:, :, h, :].rearrange("b p c -> p b c"), a, ta, t))

        k_head(0, *pair[0])
        k_head(1, *pair[1])
        for h in range(2, 8):
            ps, t = dense(N2)
            k_head(h, ps, t)
            W.done(t)
        tn = act.do(lambda e: e.activation(nk[:, :], ssk[:, :], ACT.Sqrt), t_b[7], t5)
        t = dve.do(lambda e: e.reciprocal(spl[:, :], nk[:, :]), tn)
        t = mult(spl[:, :], spl[:, :], ssk[:, :], t)
        t = dve.do(lambda e: e.tensor_tensor(nk[:, :], nk[:, :], spl[:, :], ALU.add), t)
        t_nk = dve.do(lambda e: e.tensor_scalar(nk[:, :], nk[:, :], 0.5, None, op0=ALU.mult), t)

        free = [(q.sem, q.count) for q in (pe, act, dve, pool)]
        NB = at(177.3125, [2, 32, 32])
        UB = at(185.3125, [2, 32, 32])
        PB = at(193.3125, [2048])
        s_nb = sem("s_nb")
        for hf in range(2):
            for k in range(2):
                o = 64 * hf + 32 * k
                t_nb = sp.dma(NB[64 * hf:64 * hf + 64, k, :, :], LTD[:, o:o + 32, o:o + 32], s_nb,
                              *free, *t_lt)
        t_u = dve.do(lambda e: e.memset(UB[:, :, :, :], 0.0), *free)
        t_u = dve.do(lambda e: e.memset(
            UB[:, :, :, :].rearrange("p k a b -> p k (a b)")[:, :, ::33], 1.0), t_u)
        box = {"u": t_u, "p": t_u}

        def substitute(j):
            n = 31 - j
            pb = PB[:, 0:2 * n * n].rearrange("p (k c i) -> p k c i", k=2, c=n)
            box["p"] = dve.do(lambda e: e.tensor_tensor(
                pb, UB[:, :, j + 1:32, j + 1:32].rearrange("p k i c -> p k c i"),
                NB[:, :, j:j + 1, j + 1:32].broadcast_to([128, 2, n, n]), ALU.mult),
                t_nb, box["u"], box["p"])
            box["u"] = box["p"] = dve.do(lambda e: e.tensor_reduce(
                UB[:, :, j, j + 1:32], pb, AX.X, ALU.add), box["p"])

        q_todo = [lambda j=j: substitute(j) for j in range(30, -1, -1)]
        cost = [(31 - j) ** 2 for j in range(30, -1, -1)]

        t_qt, t_qk = [], []

        def q_head(h, ps, t):
            kt, f = TMP.take()
            t_k = sp.dma(kt[:, :].rearrange("p (b c) -> p b c", b=8),
                         KTD[:, :, h, :].rearrange("b p c -> p b c"), s_ktin[id(kt)], t_kt[h], *f)
            a, ta = conv_silu(h, ps, t)
            psn, t = natural(a, ta)
            PSW.put(psn, square_rows(psn, t, ssq, h)[0])
            psk, t = blocks(kt, a, ta, t_k)
            TMP.put(kt, t)
            qk, f = TMP.take()
            t2 = dve.do(lambda e: e.tensor_tensor(b3(qk[:, :]), b3(psk[:, :]), E[h][:, :, :], ALU.mult),
                        t, t_E[h], *f)
            PSW.put(psk, t2)
            t2 = pool.do(lambda e: e.tensor_tensor(
                b3(qk[:, :]), b3(qk[:, :]), TI[:, :].unsqueeze(1).broadcast_to([128, 8, 128]),
                ALU.mult), t2)
            t_qk.append(store(QKT[:, :, h, :].rearrange("b p c -> p b c"), qk, t2))
            t_qt.append(store(QTD[:, :, h, :].rearrange("b p c -> p b c"), a, ta, t))

        s_ktin = {id(t): sem(f"s_ktin{i}") for i, t in enumerate(tmps)}
        total, spent = sum(cost), 0
        for h in range(8):
            ps, t = dense(N2)
            q_head(h, ps, t)
            W.done(t)
            while q_todo and spent < total * (h + 1) / 8:
                spent += cost.pop(0)
                q_todo.pop(0)()
        t_cq = dve.do(lambda e: e.tensor_scalar(ssq[:, :], ssq[:, :], EPS, 128 * EPS,
                                                op0=ALU.add, op1=ALU.mult), (dve.sem, dve.count))

        free = [(q.sem, q.count) for q in (pe, act, dve, pool)]
        TB = at(193.3125, [2, 32, 32])
        t_tb = dve.do(lambda e: e.tensor_copy(
            TB[:, :, :, :], UB[:, :, :, :].rearrange("p k j a -> p k a j")), box["u"], box["p"])
        s_ub, s_tb = sem("s_ub"), sem("s_tb")
        t_ub = sp.dma(UBD, UB[:, 1, :, :], s_ub, box["u"])
        t_tbd = sp.dma(TBD, TB[:, 0, :, :], s_tb, t_tb)
        sp.wait(t_zero)
        s_ud, s_t64 = sem("s_ud"), sem("s_t64")
        for hf in range(2):
            for k in range(2):
                o = 64 * hf + 32 * k
                t_ud = sp.dma(UD[:, o:o + 32, o:o + 32], UB[64 * hf:64 * hf + 64, k, :, :], s_ud, box["u"])
        for k in range(2):
            t_t64 = sp.dma(T64[:, 32 * k:32 * k + 32, 32 * k:32 * k + 32], TB[0:64, k, :, :], s_t64, t_tb)

        LB = at(0, [32, 128])
        OB = at(16, [32, 128])
        RA = at(177.3125, [32, 32])
        RB = at(181.3125, [32, 32])
        t_lb = pool.do(lambda e: e.memset(LB[:, :, :], 0.0), *free)
        t_ob = pool.do(lambda e: e.memset(OB[:, :, :], 0.0), *free)
        s_lb, s_ra, s_rb = sem("s_lb"), sem("s_ra"), sem("s_rb")
        t_nbf = [t_ub, t_ud, t_tb, box["p"]]
        for q in range(4):
            p = slice(32 * q, 32 * q + 32)
            for hf in range(2):
                tl = sp.dma(LB[p, 16 * hf:16 * hf + 16, 32 * q:32 * q + 32],
                            LTD[q::4, 64 * hf:64 * hf + 32, 64 * hf + 32:64 * hf + 64].rearrange(
                                "m a b -> a m b"), s_lb, t_lb)
            tra = sp.dma(RA[p, :, :], TBD[q::4].rearrange("m a b -> a m b"), s_ra, t_tbd, *t_nbf)
            trb = sp.dma(RB[p, :, :], UBD[q::4].rearrange("m a b -> a m b"), s_rb, t_ub, *t_nbf)

        st = {}

        def join32():
            ps, f = PSW.take()
            for g in range(32):
                t = pe.do(lambda e: e.matmul(ps[:, 32 * g:32 * g + 32], LB[:, g, :], RA[:, g, :],
                                             start=True, stop=True), tl, tra, *f, mark=g == 31)
            for q in range(4):
                p = slice(32 * q, 32 * q + 32)
                t2 = dve.do(lambda e: e.tensor_copy(
                    OB[p, :, 32 * q:32 * q + 32], ps[p, :].rearrange("p (g c) -> p g c", g=32)), t, t_ob)
            PSW.put(ps, t2)
            st["o"], st["l"] = t2, t

        def join32b():
            ps, f = PSW.take()
            for g in range(32):
                t = pe.do(lambda e: e.matmul(ps[:, 32 * g:32 * g + 32], OB[:, g, :], RB[:, g, :],
                                             start=True, stop=True), st["o"], trb, *f, mark=g == 31)
            X2, XP2 = RA, at(201.3125, [4, 4, 32])
            t3 = act.do(lambda e: e.activation(
                XP2[:, :, :, :], ps[:, 0:512].rearrange("p (n m c) -> p m n c", n=4, m=4), ACT.Copy), t, *free)
            t2 = act.do(lambda e: e.activation(X2[:, :, :].rearrange("p g c -> p (g c)"), ps[:, :],
                                               ACT.Copy), t, st["l"])
            PSW.put(ps, t2)
            st["x"], st["b"], st["xp"] = t3, t, XP2
            s_x = sem("s_t21")
            for q in range(4):
                for hf in range(2):
                    st["ud"] = sp.dma(
                        UD[q::4, 64 * hf:64 * hf + 32, 64 * hf + 32:64 * hf + 64].rearrange("m a b -> a m b"),
                        X2[32 * q:32 * q + 32, 16 * hf:16 * hf + 16, :], s_x, t2)

        def join32c():
            ps, f = PSW.take()
            for m in range(4):
                t = pe.do(lambda e: e.transpose(
                    ps[:, 128 * m:128 * m + 128],
                    st["xp"][:, m, :, :].rearrange("p n c -> p (n c)"), ident[:, :]), st["x"], *f, mark=m == 3)
            X3 = at(185.3125, [4, 4, 32])
            t2 = act.do(lambda e: e.activation(X3[:, :, :, :].rearrange("p m q c -> p (m q c)"),
                                               ps[:, 0:512], ACT.Copy), t, t_ub, t_ud, t_tb)
            PSW.put(ps, t2)
            s_x = sem("s_t21n")
            for m4 in range(4):
                st["t64"] = sp.dma(
                    T64[16 * m4:16 * m4 + 16, 32:64, 0:32].rearrange("n a b -> a n b"),
                    X3[32 * m4:32 * m4 + 32, :, :, :].rearrange("p m q c -> p (m q) c"), s_x, t2)
            st["c"] = t

        def load64():
            fr = [st["ud"], st["t64"], st["b"], st["c"], st["o"]]
            t1 = pool.do(lambda e: e.memset(LB[:, :, :], 0.0), *fr)
            st["ob"] = pool.do(lambda e: e.memset(OB[:, :, :], 0.0), *fr)
            s_l, s_r, s_u = sem("s_l64"), sem("s_r64"), sem("s_u64")
            st["ra"], st["rb"] = at(177.3125, [32, 64]), at(185.3125, [32, 64])
            for q in range(2):
                p = slice(64 * q, 64 * q + 64)
                st["tl"] = sp.dma(LB[p, :, 64 * q:64 * q + 64],
                                  LTD[q::2, 0:64, 64:128].rearrange("m a b -> a m b"), s_l, t1)
                st["tra"] = sp.dma(st["ra"][p, :, :], T64[q::2].rearrange("m a b -> a m b"), s_r,
                                   st["t64"], t_t64, *fr)
                st["trb"] = sp.dma(st["rb"][p, :, :],
                                   UD[q::2, 64:128, 64:128].rearrange("m a b -> a m b"), s_u,
                                   st["ud"], t_ud, *fr)

        def join64(n):
            ps, f = PSW.take()
            for g in range(16):
                t = pe.do(lambda e: e.matmul(ps[:, 64 * g:64 * g + 64], LB[:, 16 * n + g, :],
                                             st["ra"][:, 16 * n + g, :], start=True, stop=True),
                          st["tl"], st["tra"], *f, mark=g == 15)
            for q in range(2):
                p = slice(64 * q, 64 * q + 64)
                t2 = dve.do(lambda e: e.tensor_copy(
                    OB[p, 16 * n:16 * n + 16, 64 * q:64 * q + 64],
                    ps[p, :].rearrange("p (g c) -> p g c", g=16)), t, st["ob"])
            PSW.put(ps, t2)
            st["j", n] = t2

        def join64b(n):
            ps, f = PSW.take()
            for g in range(16):
                t = pe.do(lambda e: e.matmul(ps[:, 64 * g:64 * g + 64], OB[:, 16 * n + g, :],
                                             st["rb"][:, 16 * n + g, :], start=True, stop=True),
                          st["j", n], st["trb"], *f, mark=g == 15)
            x = at(193.3125 + 4 * n, [16, 64])
            t2 = act.do(lambda e: e.activation(x[:, :, :].rearrange("p g c -> p (g c)"), ps[:, :],
                                               ACT.Copy), t, t_tbd, t_t64)
            PSW.put(ps, t2)
            s_x = sem(f"s_t64_{n}")
            for q in range(2):
                st["u", n] = sp.dma(
                    UD[32 * n + q:32 * n + 32:2, 0:64, 64:128].rearrange("m a b -> a m b"),
                    x[64 * q:64 * q + 64, :, :], s_x, t2)

        joins = {0: join32, 1: join32b, 2: lambda: (join32c(), load64()), 4: lambda: join64(0),
                 5: lambda: (join64(1), join64b(0)), 6: lambda: join64b(1)}
        t_vp = []
        for h in range(8):
            ps, t = dense(N2)
            a, ta = conv_silu(16 + h, ps, t)
            W.done(t)
            psn, t = natural(a, ta)
            TMP.put(a, t)
            vp, f = TMP.take()
            t1 = dve.do(lambda e: e.tensor_tensor(b3(vp[:, :]), b3(psn[:, :]), per_row(nk, h),
                                                  ALU.mult), t, t_nk, *f)
            PSW.put(psn, t1)
            t_vp.append(store(VPD[:, :, h, :].rearrange("b p c -> p b c"), vp, t1))
            if h in joins:
                joins[h]()
        t_gt = []
        for h in range(8):
            ps, t_gate = dense(N2)
            g, f = TMP.take()
            t = mult(g[:, :], ps[:, :], INV[:, :], t_gate, N2.t_inv, *f)
            PSW.put(ps, t)
            t = act.do(lambda e: e.activation(g[:, :], g[:, :], ACT.Silu), t)
            W.done(t_gate)
            t_gt.append(store(GTD[:, :, h, :].rearrange("b p c -> p b c"), g, t))

        end = [(q.sem, q.count) for q in (pe, act, dve, pool)]
        s_h = sem("s_hback")
        for m in range(KT):
            t_h[m] = sp.dma(H[:, m, :], HD[m], s_h, t_hd, *end)
        t_h = [t_h[7]] * KT
        STEP = Slots([])
        for i in range(2):
            STEP.put(([at(32 + 28 * i + 4 * k, [8, 128]) for k in range(7)],
                      [sem(f"s_step{i}_{k}") for k in range(7)]), t_gate)
        SS = Slots([])
        for kb in (88, 92):
            SS.put([at(kb + 0.5 * h, [128]) for h in range(8)], t_gate)
        ring_free = [(s_tmp[id(t)], sp.counts.get(s_tmp[id(t)], 0)) for t in tmps] + \
            [tok for _, f in TMP.line for tok in f] + [st["u", 0], st["u", 1]] + end
        at0 = 145.25
        RV, VN, O1, O2, SQ, YT = (Slots([]) for _ in range(6))
        RV.put(at(at0, [8, 128]), *ring_free)
        VN.put(at(at0 + 4, [8, 128]), *ring_free)
        O1.put(at(at0 + 8, [8, 128]), *ring_free)
        O2.put(at(at0 + 12, [8, 128]), *ring_free)
        SQ.put(at(at0 + 16, [8, 128]), *ring_free)
        YU = Slots([])
        for i in range(2):
            YU.put((at(at0 + 20 + 16 * i, [8, 256], F32R), at(at0 + 28 + 16 * i, [8, 256], F32R)),
                   *ring_free)
        YT.put(at(at0 + 52, [8, 128]), *ring_free)
        BK = Slots([(ps, n) for ps in psum for n in range(2)])
        BK.line = []
        for ps in psum:
            f = next(f for b, f in PSW.line if b is ps)
            for n in range(2):
                BK.put((ps, n), *f)

        def load_step(b):
            (bufs, sems), f = STEP.take()
            srcs = ((KTD, t_kt), (KDD, t_kd), (QTD, t_qt), (QKT, t_qk), (VPD, t_vp),
                    (None, [st["u", 0], st["u", 1], st["ud"], t_ud]), (GTD, t_gt))
            toks = []
            for i, (src, tk) in enumerate(srcs):
                ap = UD[8 * b:8 * b + 8].rearrange("h j i -> j h i") if src is None else src[b]
                toks.append(sp.dma(bufs[i][:, :, :], ap, sems[i], *f, *tk))
            return bufs, sems, toks

        def col(t, b, h):
            return t[:, 8 * b + h:8 * b + h + 1]

        def four(b, g, fn, *after):
            bk, f = BK.take()
            ps = bank(bk)
            for i in range(4):
                l, r = fn(4 * g + i)
                t = pe.do(lambda e: e.matmul(ps[:, 128 * i:128 * i + 128], l, r, start=True, stop=True),
                          *after, *f, mark=i == 3)
            return bk, ps, t

        og = vec[:, 80:81]
        fa, fb, fs = var2, ivf, spl
        steps = {0: load_step(0)}
        S_now = None
        y_unit = None
        w_atoms = []
        box = {"f": []}

        def out_atoms2(n, units, hook=None):
            hold = []

            def atom(m):
                wh, wl, th, tl = W.get()
                bk, f = BK.take()
                ps = bank(bk)
                for u, (yh, yl, t1, t2) in enumerate(units):
                    for k in range(8):
                        for i, (l, r) in enumerate(((wh, yh), (wl, yh), (wh, yl))):
                            end_ = k == 7 and i == 2
                            t = pe.do(lambda e: e.matmul(
                                ps[:, 256 * u:256 * u + 256], l[:, 128 * k:128 * k + 128], r[:, k, :],
                                start=k == 0 and i == 0, stop=end_),
                                *(th + f + t1 if i == 0 else tl + t2), mark=end_ and u == 1)
                c = slice(512 * n, 512 * n + 512)
                t_h[m] = dve.do(lambda e: e.tensor_tensor(H[:, m, c], H[:, m, c], ps[:, :], ALU.add),
                                t, t_h[m])
                BK.put(bk, t_h[m])
                W.done(t)
                if m == 7:
                    for yh, yl, _, _ in units:
                        YU.put((yh, yl), t)
                if hook:
                    hook(m)
            return [lambda m=m: atom(m) for m in range(8)]

        units = []
        for b in range(8):
            bufs, sems, toks = steps.pop(b)
            KTb, KDb, QTb, QKb, VPb, Ub, Gb = bufs
            if b < 7:
                steps[b + 1] = load_step(b + 1)
            filler = w_atoms[:]
            del w_atoms[:]

            def fill(n):
                for _ in range(n):
                    if filler:
                        filler.pop(0)()

            rv, rf = RV.take()
            vn, vf = VN.take()
            o1, o1f = O1.take()
            o2, o2f = O2.take()
            S_new, sf = SS.take() if b < 7 else (None, [])
            t_s = {}
            ks, x1, xx = {}, {}, {}
            for g in range(2):
                if b:
                    ks[g] = four(b, g, lambda h: (KTb[:, h, :], S_now[0][h][:, :]), toks[0], *S_now[1][g])
                    x1[g] = four(b, g, lambda h: (QTb[:, h, :], S_now[0][h][:, :]), toks[2], *S_now[1][g])
            t_r, t_o1 = [toks[4]] * 2, [None] * 2
            if b:
                for g in range(2):
                    bk, ps, t = ks[g]
                    for i in range(4):
                        h = 4 * g + i
                        t_r[g] = dve.do(lambda e: e.scalar_tensor_tensor(
                            rv[:, h, :], ps[:, 128 * i:128 * i + 128], col(eGn, b, h), VPb[:, h, :],
                            op0=ALU.mult, op1=ALU.add), t, toks[4], t_egn, *rf)
                    BK.put(bk, t_r[g])
            src = rv if b else VPb
            t_v = [None] * 2
            for g in range(2):
                bk, ps, t = four(b, g, lambda h: (Ub[:, h, :], src[:, h, :]), toks[5], t_r[g])
                for i in range(4):
                    h = 4 * g + i
                    t_v[g] = act.do(lambda e: e.activation(
                        vn[:, h, :], ps[:, 128 * i:128 * i + 128], ACT.Copy, scale=col(bc, b, h)),
                        t, *t_b, *vf)
                BK.put(bk, t_v[g])
                if g == 0 and b:
                    for gg_ in range(2):
                        bk1, ps1, t1 = x1[gg_]
                        for i in range(4):
                            h = 4 * gg_ + i
                            t_o1[gg_] = act.do(lambda e: e.activation(
                                o1[:, h, :], ps1[:, 128 * i:128 * i + 128], ACT.Copy, scale=col(eG, b, h)),
                                t1, t_eg, *o1f)
                        BK.put(bk1, t_o1[gg_])
            RV.put(rv, t)
            t_sn = [None] * 2
            t_o2 = [None] * 2
            for g in range(2):
                if b < 7:
                    bk, ps, t = four(b, g, lambda h: (KDb[:, h, :], vn[:, h, :]), toks[1], t_v[g])
                    for i in range(4):
                        h = 4 * g + i
                        pb_ = ps[:, 128 * i:128 * i + 128]
                        if b:
                            t_sn[g] = dve.do(lambda e: e.scalar_tensor_tensor(
                                S_new[h][:, :], S_now[0][h][:, :], col(eGL, b, h), pb_,
                                op0=ALU.mult, op1=ALU.add), t, t_eg, *S_now[1][g], *sf)
                        else:
                            t_sn[g] = dve.do(lambda e: e.tensor_copy(S_new[h][:, :], pb_), t, *sf)
                    BK.put(bk, t_sn[g])
                bk, ps, t = four(b, g, lambda h: (QKb[:, h, :], vn[:, h, :]), toks[3], t_v[g])
                hs = slice(4 * g, 4 * g + 4)
                o2g = o2[:, hs, :]
                p3 = ps.rearrange("p (h c) -> p h c", h=4)
                if b:
                    t_o2[g] = dve.do(lambda e: e.tensor_tensor(o2g, p3, o1[:, hs, :], ALU.add),
                                     t, t_o1[g], *o2f)
                else:
                    t_o2[g] = dve.do(lambda e: e.tensor_copy(o2g, p3), t, *o2f)
                BK.put(bk, t_o2[g])
                t_vnf = t
            VN.put(vn, t_vnf)
            O1.put(o1, t_o2[1])
            if S_now:
                SS.put(S_now[0], t_vnf, *[x for x in t_sn if x])
            S_now = (S_new, [[t_sn[0]], [t_sn[1]]]) if b < 7 else None
            fill(4)
            sq, f = SQ.take()
            t = act.do(lambda e: e.activation(sq[:, :, :], o2[:, :, :], ACT.Square), *t_o2, *f)
            c8 = slice(8 * b, 8 * b + 8)
            t = dve.do(lambda e: e.tensor_reduce(fa[:, 0:8], sq[:, :, :], AX.X, ALU.add), t, *box["f"])
            SQ.put(sq, t)
            t = dve.do(lambda e: e.scalar_tensor_tensor(fa[:, 0:8], fa[:, 0:8], 1.0 / 128, ssq[:, c8],
                                                        op0=ALU.mult, op1=ALU.add), t, t_cq)
            t = inv_sqrt(fb[:, 0:8], fa[:, 0:8], fs[:, 0:8], t)
            box["f"] = [t]
            t_on = pool.do(lambda e: e.tensor_tensor(
                o2[:, :, :], o2[:, :, :], fb[:, 0:8].unsqueeze(2).broadcast_to([128, 8, 128]),
                ALU.mult), t)
            box["f"] = [t_on]
            fill(8)
            if b % 2 == 0:
                y_unit, yf = YU.take()
            yt, f = YT.take()
            for g in range(2):
                bk, fk = BK.take()
                ps = bank(bk)
                for i in range(4):
                    t = pe.do(lambda e: e.transpose(ps[:, 128 * i:128 * i + 128], o2[:, 4 * g + i, :],
                                                    ident[:, :]), t_on, *fk, mark=i == 3)
                hs = slice(4 * g, 4 * g + 4)
                t_y = dve.do(lambda e: e.scalar_tensor_tensor(
                    yt[:, hs, :], ps.rearrange("p (h c) -> p h c", h=4), og, Gb[:, hs, :],
                    op0=ALU.mult, op1=ALU.mult), t, toks[6], t_const, *f)
                BK.put(bk, t_y)
            O2.put(o2, t)
            STEP.put((bufs, sems), t_y, t_vnf)
            c = slice(128 * (b % 2), 128 * (b % 2) + 128)
            t1, t2 = split(yt[:, :, :], y_unit[0][:, :, c], y_unit[1][:, :, c], t_y, *yf)
            YT.put(yt, t1, t2)
            if b % 2 == 0:
                yt1, yt2 = [t1], [t2]
            else:
                units.append((y_unit[0], y_unit[1], yt1 + [t1], yt2 + [t2]))
                if b % 4 == 3:
                    w_atoms += out_atoms2(b // 4, units)
                    units = []
        for fn in w_atoms:
            fn()
        if upto == 4:
            return finish()

        end = [(q.sem, q.count) for q in (pe, act, dve, pool)]
        PSW = Slots([])
        for ps in psum:
            PSW.put(ps, *[tok for (b, _), f in BK.line if b is ps for tok in f])
        ACC = [at(139 + 4 * i, [S]) for i in range(8)]
        TMP = Slots([])
        TMP.put(at(203, [S]), *end)
        for b in ACC:
            TMP.put(b, *end)
        RH = [at(171 + 8 * i, [S], F32R) for i in range(4)]
        RL = [at(175 + 8 * i, [S], F32R) for i in range(4)]
        N3 = Norm(vec[:, 64:72])
        for k in range(8):
            N3.feed(k, t_h[k], *end)

        def square_relu(ps, t, i, *free):
            r, f = TMP.take()
            t = act.do(lambda e: e.activation(r[:, :], ps[:, :], ACT.Relu), t, *f)
            PSW.put(ps, t)
            t = act.do(lambda e: e.activation(r[:, :], r[:, :], ACT.Square), t)
            t1, t2 = split(r[:, :], RH[i][:, :], RL[i][:, :], t, *free)
            TMP.put(r, t1, t2)
            return [t1], [t2]

        pair = dense_pair(N3)
        ps, f = PSW.take()
        t = mean_eps(var[:, :], ps[:, 0:8], N3.sq.columns(ps, f))
        PSW.put(ps, t)
        t = dve.do(lambda e: e.reciprocal(invc[:, :], var[:, :]), t)
        t_inv2 = spread(invc, INV[:, :], t)
        rs = [None] * 4
        for i in range(2):
            W.done(pair[i][1])
            rs[i] = square_relu(*pair[i], i, *end)
        acc_free = [tok for _, f in TMP.line for tok in f]
        TMP.line = [(b, f) for b, f in TMP.line if b not in ACC]
        t_acc = [acc_free] * 8
        SQF = Squares()
        for g in range(8):
            for i in range(4):
                if rs[i] is None:
                    ps, t = dense(N3)
                    W.done(t)
                    rs[i] = square_relu(ps, t, i, *rfree) if g else square_relu(ps, t, i, *end)
            ahead = None
            if g == 7:
                for i in range(6):
                    TMP.put(at(32 + 4 * i, [S]), t)
            if g < 7:
                ahead = dense(N3)
                W.done(ahead[1])
            for j in range(4):
                wh, wl, th, tl = W.get()
                for x in range(2):
                    m = 2 * j + x
                    ps, free = PSW.take()
                    o = 512 * x
                    t = product(ps, [(wh[:, o + 128 * k:o + 128 * k + 128], wl[:, o + 128 * k:o + 128 * k + 128],
                                      RH[k], RL[k], th + rs[k][0] + free, tl + rs[k][1])
                                     for k in range(4)])
                    if g == 0:
                        t_acc[m] = [act.do(lambda e: e.activation(ACC[m][:, :], ps[:, :], ACT.Copy),
                                           t, *t_acc[m])]
                    else:
                        t_acc[m] = [dve.do(lambda e: e.tensor_tensor(
                            ACC[m][:, :], ACC[m][:, :], ps[:, :], ALU.add), t, *t_acc[m])]
                    PSW.put(ps, *t_acc[m])
                    if g == 7:
                        ta = mult(ACC[m][:, :], ACC[m][:, :], INV[:, :], *t_acc[m], t_inv2)
                        t_h[m] = dve.do(lambda e: e.tensor_tensor(H[:, m, :], H[:, m, :], ACC[m][:, :],
                                                                  ALU.add), ta, t_h[m])
                        SQF.feed(H[:, m, :], t_h[m])
                W.done(t)
            rfree = [t]
            rs = [None] * 4
            if ahead:
                rs[0] = square_relu(*ahead, 0, *rfree)
        if upto == 5:
            return finish()

        ps, f = PSW.take()
        t = mean_eps(var[:, :], ps[:, 0:8], SQF.columns(ps, f))
        PSW.put(ps, t)
        t = inv_sqrt(invc[:, :], var[:, :], sd[:, :], t)
        t_i = spread(invc, INV[:, :], t, free=[ta])
        s_out = [sem(f"s_out{m}") for m in range(8)]
        outs = []
        for m in range(KT):
            t = dve.do(lambda e: e.scalar_tensor_tensor(
                H[:, m, :], H[:, m, :], vec[:, 72 + m:73 + m], INV[:, :], op0=ALU.mult, op1=ALU.mult),
                t_i, SQF.t, t_h[m])
            outs.append(sp.dma(out[128 * m:128 * m + 128, :], H[:, m, :], s_out[m], t))
        sp.wait(*outs)


def lay_out(inputs):
    def tiles(w, kb, mb):
        k, m = w.shape
        t = w.reshape(k // (128 * kb), kb, 128, m // (128 * mb), mb, 128)
        return np.ascontiguousarray(t.transpose(0, 3, 2, 4, 1, 5)).reshape(-1, 128, 1024)

    def cols(v):
        return v.reshape(-1, 128).T

    f = {k: np.asarray(v) for k, v in inputs.items()}
    count = 1.0 / np.arange(1, 17, dtype=np.float32)
    A = {
        "xT": np.ascontiguousarray(f["x"][0].T),
        "ident": np.eye(128, dtype=np.float32),
        "vec": np.ascontiguousarray(np.concatenate([
            cols(f["norm_g"][0]), np.broadcast_to(count, (128, 16)), cols(f["pool_scale"][0]),
            cols(f["norm_g"][1]), cols(f["norm_f"]), cols(f["norm_mix_g_2"][0]),
            cols(f["norm_mlp_g_2"][0]), cols(f["final_norm_g_2"]), cols(f["gdn_o_norm_g_2"][0]),
        ], axis=1)),
        "pool_in": tiles(f["pool_w_in"][0], 8, 1),
        "pool_g": np.concatenate([tiles(f["pool_w"][0, g], 4, 2) for g in range(4)]),
        "pool_out": tiles(f["pool_w_out"][0], 2, 4),
    }
    A["sb_in"] = tiles(f["sb_w_in"][0], 8, 1)
    wv = f["sb_w_in"][0][:, 2048:4096].reshape(4, 2, 128, 4, 512)
    A["sb_v"] = np.ascontiguousarray(wv.transpose(3, 0, 2, 1, 4)).reshape(16, 128, 1024)
    A["sb_out"] = tiles(f["sb_w_out"][0], 2, 4)
    mask = np.where(np.arange(128)[None, :] < np.arange(128)[:, None], 0.0, -1e30)
    A["mask"] = mask.astype(np.float32)
    i = np.arange(128)
    A["tri_incl"] = (i[:, None] <= i[None, :]).astype(np.float32)
    A["tri_strict"] = (i[:, None] > i[None, :]).astype(np.float32)
    gw = f["gdn_w_in_2"][0]
    A["gdn_in"] = tiles(np.ascontiguousarray(gw[:, 0:4096]), 8, 1)
    A["gdn_ab"] = np.ascontiguousarray(gw[:, 4096:4112].reshape(8, 128, 16).transpose(1, 0, 2)).reshape(128, 128)
    A["gdn_vec"] = np.ascontiguousarray(np.concatenate([
        f["gdn_conv_w_2"][0].reshape(4, 24, 128).transpose(2, 1, 0).reshape(128, 96),
        np.broadcast_to(f["gdn_a_log_2"][0], (128, 8)), np.broadcast_to(f["gdn_dt_bias_2"][0], (128, 8)),
    ], axis=1))
    A["gdn_out"] = tiles(f["gdn_w_out_2"][0], 8, 1)
    A["w1"] = tiles(f["mlp_w1_2"][0], 8, 1)
    A["w2"] = tiles(f["mlp_w2_2"][0], 4, 2)
    return A


def kernel(**inputs):
    import concourse.bacc as bacc
    from concourse.bass_utils import run_bass_kernel_spmd

    A = lay_out(inputs)
    nc = bacc.Bacc("TRN2", target_bir_lowering=False, num_devices=1)
    args = {k: nc.dram_tensor("in_" + k, v.shape, mybir.dt.from_np(v.dtype), kind="ExternalInput").ap()
            for k, v in A.items()}
    out = nc.dram_tensor("out", (D, S), F32, kind="ExternalOutput").ap()
    program(nc, args, out)
    r = run_bass_kernel_spmd(nc, [{"in_" + k: v for k, v in A.items()}], core_ids=[0])
    return np.ascontiguousarray(r.results[0]["out"].T)[None]
```

```python
from contextlib import ExitStack

import numpy as np

import concourse.bass as bass
from concourse import mybir

F32 = mybir.dt.float32
F32R = mybir.dt.float32r
ALU = mybir.AluOpType
ACT = mybir.ActivationFunctionType
AX = mybir.AxisListType

S = 1024
D = 1024
KT = 8
EPS = 1e-6
KB = 1024


class Queue:

    def __init__(self, engine, sem):
        self.engine, self.sem, self.count, self.seen = engine, sem, 0, {}

    def wait(self, *after):
        for sem, n in after:
            if self.seen.get(sem, 0) < n:
                self.seen[sem] = n
                self.engine.wait_ge(sem, n)

    def do(self, fn, *after, mark=True):
        self.wait(*after)
        ins = fn(self.engine)
        if mark:
            ins.then_inc(self.sem, 1)
            self.count += 1
        return self.sem, self.count


class Loader(Queue):

    def __init__(self, engine):
        super().__init__(engine, None)
        self.counts = {}

    def dma(self, dst, src, sem, *after):
        self.wait(*after)
        self.engine.dma_start(dst.bitcast(F32), src.bitcast(F32)).then_inc(sem, 16)
        self.counts[sem] = self.counts.get(sem, 0) + 16
        return sem, self.counts[sem]


class Slots:

    def __init__(self, bufs, free=()):
        self.line = [(b, list(free)) for b in bufs]

    def take(self):
        return self.line.pop(0)

    def put(self, buf, *tokens):
        self.line.append((buf, list(tokens)))


def program(nc, A, out):
    ctx = ExitStack()
    with ctx:
        base = (nc.sbuf_base + 31) // 32 * 32
        arena = ctx.enter_context(nc.sbuf_tensor("arena", [128, 53200], F32))
        names = [0]

        def at(kb, shape, dt=F32):
            names[0] += 1
            return nc.alloc_sbuf_tensor_at(f"m{names[0]}", [128] + shape, dt,
                                           offset=base + int(kb * KB))

        def sem(name):
            return ctx.enter_context(nc.semaphore(name))

        pe = Queue(nc.tensor, sem("pe"))
        dve = Queue(nc.vector, sem("dve"))
        act = Queue(nc.scalar, sem("act"))
        pool = Queue(nc.gpsimd, sem("pool"))
        sp = Loader(nc.sync)

        psum = [ctx.enter_context(nc.psum_tensor(f"ps{i}", [128, 1024], F32)) for i in range(4)]
        PSW = Slots(psum)

        H = at(0, [KT, S])
        UH = at(32, [KT, S], F32R)
        UL = at(64, [KT, S], F32R)
        STG = [at(96 + 4 * i, [1024]) for i in range(3)]
        WH = [at(108 + 8 * i, [1024], F32R) for i in range(3)]
        WL = [at(112 + 8 * i, [1024], F32R) for i in range(3)]
        INV = at(132, [S])
        ident = at(136, [128])
        ones = at(136.5, [128])
        vec = at(137, [128])
        identr = at(137.5, [128], F32R)
        maskr = at(138, [128], F32R)
        invc = at(138.5, [8])
        sd = at(138.53125, [8])
        var = at(138.65625, [8])
        EDGE = at(138.59375, [16])
        WORK = 139

        s_vec, s_ident = sem("s_vec"), sem("s_ident")
        t_const = sp.dma(vec[:, 0:A["vec"].shape[1]], A["vec"], s_vec)
        t_ones = pool.do(lambda e: e.memset(ones[:, :], 1.0))


        def mult(dst, a, b, *after, q=dve):
            return q.do(lambda e: e.tensor_tensor(dst, a, b, ALU.mult), *after)

        def split(src, hi, lo, *after, q=act, ql=dve):
            t = q.do(lambda e: e.activation(hi, src, ACT.Copy), *after) if q is act else \
                q.do(lambda e: e.tensor_scalar(hi, src, 1.0, 0.0, op0=ALU.mult, op1=ALU.add), *after)
            u = ql.do(lambda e: e.tensor_tensor(lo, src, hi.bitcast(F32), ALU.subtract), t, *after)
            return t, u

        def product(ps, terms, *after, begin=True, finish_=True):
            last = len(terms) - 1
            for k, (wh, wl, ah, al, th, tl) in enumerate(terms):
                for i, (l, r) in enumerate(((wh, ah), (wl, ah), (wh, al))):
                    for n in range(2):
                        end = k == last and i == 2
                        first = k == 0 and i == 0 and begin
                        t = pe.do(
                            lambda e, l=l, r=r, n=n, first=first, end=end and finish_:
                            e.matmul(ps[:, 512 * n:512 * n + 512], l, r[:, 512 * n:512 * n + 512],
                                     start=first, stop=end),
                            *(after + tuple(th) if i == 0 else tuple(tl)), mark=end and n == 1)
            return t


        class Weights:
            def __init__(self):
                self.q, self.ql = act, dve
                self.plan, self.loaded, self.used, self.hi, self.lo, self.use = [], [], 0, [], [], []
                self.sems = [sem(f"s_stage{i}") for i in range(3)]

            def add(self, name, tiles):
                self.plan += [A[name][i] for i in tiles]

            def load(self):
                n = len(self.loaded)
                if n < len(self.plan):
                    freed = (self.hi[n - 3], self.lo[n - 3]) if n >= 3 else ()
                    self.loaded.append(sp.dma(STG[n % 3][:, :], self.plan[n], self.sems[n % 3], *freed))

            def split(self):
                n = len(self.hi)
                if n < len(self.plan):
                    freed = (self.use[n - 3],) if n >= 3 else ()
                    t, u = split(STG[n % 3][:, :], WH[n % 3][:, :], WL[n % 3][:, :],
                                 self.loaded[n], *freed, q=self.q, ql=self.ql)
                    self.hi.append(t)
                    self.lo.append(u)
                    self.load()

            def split_into(self, hi, lo, *free):
                n = len(self.hi)
                t, u = split(STG[n % 3][:, :], hi[:, :], lo[:, :], self.loaded[n], *free, q=self.q)
                self.hi.append(t)
                self.lo.append(u)
                self.load()
                return [t], [u]

            def get(self):
                n = self.used
                self.used += 1
                return WH[n % 3], WL[n % 3], [self.hi[n]], [self.lo[n]]

            def done(self, t):
                self.use.append(t)
                self.split()

        W = Weights()
        W.add("pool_in", [0])
        for g in range(4):
            W.add("pool_in", [4 * g + 1, 4 * g + 2, 4 * g + 3, 16 + 4 * g, 17 + 4 * g])
            W.add("pool_g", [2 * g])
            W.add("pool_in", [18 + 4 * g])
            W.add("pool_out", [4 * g, 4 * g + 1])
            W.add("pool_in", [19 + 4 * g])
            W.add("pool_g", [2 * g + 1])
            if g < 3:
                W.add("pool_in", [4 * g + 4])
            W.add("pool_out", [4 * g + 2, 4 * g + 3])

        for i in range(8):
            W.add("sb_in", [i, 8 + i])
        W.add("sb_v", range(16))
        W.add("sb_in", range(32, 48))
        W.add("sb_out", range(16))
        W.add("gdn_in", [8 + i for i in range(8)] + [i for i in range(8)] + list(range(16, 32)))
        W.add("gdn_out", range(8))
        LAST = (0, 5, 6, 7, 1, 2, 3, 4)
        W.add("gdn_out", LAST)
        W.add("w1", range(4))
        for g in range(8):
            if g < 7:
                W.add("w1", [4 * g + 4])
            W.add("w2", range(4 * g, 4 * g + 4))
            if g < 7:
                W.add("w1", [4 * g + 5, 4 * g + 6, 4 * g + 7])

        P = [at(WORK + 8 * i, [2, S]) for i in range(4)]
        PH = [at(WORK + 8 * i, [S], F32R) for i in range(4)]
        PL = [at(WORK + 8 * i + 4, [S], F32R) for i in range(4)]
        YH = [at(WORK + 32 + 8 * i, [S], F32R) for i in range(2)]
        YL = [at(WORK + 32 + 8 * i + 4, [S], F32R) for i in range(2)]
        XP = at(WORK + 48, [1040])
        tmps = [at(WORK + 52.0625 + 4.0625 * i, [1040]) for i in range(4)]
        TMP = Slots(tmps)

        s_x = [sem(f"s_x{k}") for k in range(KT)]
        t_h = []
        for k in range(KT):
            t_h.append(sp.dma(H[:, k, :], A["xT"][128 * k:128 * k + 128, :], s_x[k]))
            if k < 3:
                W.load()
        t_ident = sp.dma(ident[:, :], A["ident"], s_ident)

        def column_sums(ps, acc, t_acc, free):
            for j in range(8):
                t = pe.do(lambda e: e.matmul(
                    ps[:, j:j + 1], acc[:, 128 * j:128 * j + 128], ones[:, 0:1],
                    start=True, stop=True), t_acc, t_ones, *free, mark=j == 7)
            TMP.put(acc, t)
            return t

        class Squares:

            def __init__(self, weights=None):
                self.acc, self.weights, self.read = None, weights, []

            def feed(self, k, x, *after, q=pool):
                sq, free = TMP.take()
                t = act.do(lambda e: e.activation(sq[:, 0:S], x, ACT.Square), *after, *free)
                first = self.acc is None
                if first:
                    self.acc, self.t = sq, t
                else:
                    self.t = q.do(lambda e: e.tensor_tensor(
                        self.acc[:, 0:S], self.acc[:, 0:S], sq[:, 0:S], ALU.add), t, self.t, *self.read)
                    self.read = []
                done = [self.t]
                if self.weights is not None:
                    w, t_w = self.weights
                    w = w[:, k:k + 1]
                    if first:
                        self.acc2, f = TMP.take()
                        self.t2 = dve.do(lambda e: e.tensor_scalar(
                            self.acc2[:, 0:S], sq[:, 0:S], w, None, op0=ALU.mult), t, t_w, *f)
                        self.read = [self.t2]
                    else:
                        self.t2 = dve.do(lambda e: e.scalar_tensor_tensor(
                            self.acc2[:, 0:S], sq[:, 0:S], w, self.acc2[:, 0:S],
                            op0=ALU.mult, op1=ALU.add), t, self.t2)
                        done.append(self.t2)
                if not first:
                    TMP.put(sq, *done)

            def columns(self, ps, free):
                return column_sums(ps, self.acc, self.t, free)

            def columns2(self, ps, free):
                return column_sums(ps, self.acc2, self.t2, free)

        def inv_sqrt(dst, var, sd, *after):
            t_sd = act.do(lambda e: e.activation(sd, var, ACT.Sqrt), *after)
            t = dve.do(lambda e: e.reciprocal(sd, sd), t_sd)
            t = mult(var, var, sd, t)
            t = mult(var, var, sd, t)
            t = dve.do(lambda e: e.tensor_scalar(var, var, -0.5, 1.5, op0=ALU.mult, op1=ALU.add), t)
            return mult(dst, var, sd, t)

        def diagonals(col, *after):
            dg, f = TMP.take()
            t = dve.do(lambda e: e.tensor_tensor(
                dg[:, 0:S].rearrange("p (b c) -> p b c", b=8),
                ident[:, :].unsqueeze(1).broadcast_to([128, 8, 128]),
                col[:, 0:8].unsqueeze(2).broadcast_to([128, 8, 128]), ALU.mult), *after, t_ident, *f)
            return dg, t

        def spread(dgt, dst, free=()):
            dg, t = dgt
            ps, f = PSW.take()
            for n in range(2):
                t = pe.do(lambda e: e.matmul(
                    ps[:, 512 * n:512 * n + 512], ones[:, :], dg[:, 512 * n:512 * n + 512],
                    start=True, stop=True), t, t_ones, *f, mark=n == 1)
            TMP.put(dg, t)
            t = act.do(lambda e: e.activation(dst, ps[:, :], ACT.Copy), t, *free)
            PSW.put(ps, t)
            return t

        def mean_eps(dst, ps, *after):
            return dve.do(lambda e: e.tensor_scalar(dst, ps, 1.0 / D, EPS, op0=ALU.mult, op1=ALU.add),
                          *after)

        class Norm:

            def __init__(self, gains, weights=None):
                self.gains = gains
                self.uh, self.ul = [None] * KT, [None] * KT
                self.sq = Squares(weights)

            def high(self, k, t_h, *free):
                self.uh[k] = [act.do(lambda e: e.activation(
                    UH[:, k, :], H[:, k, :], ACT.Copy, scale=self.gains[:, k:k + 1]), t_h, t_const, *free)]

            def low(self, k, t_h, *free):
                self.ul[k] = [dve.do(lambda e: e.scalar_tensor_tensor(
                    UL[:, k, :], H[:, k, :], self.gains[:, k:k + 1], UH[:, k, :].bitcast(F32),
                    op0=ALU.mult, op1=ALU.subtract), t_h, *self.uh[k], *free)]

            def split(self, k, t_h, *free):
                self.high(k, t_h, *free)
                self.low(k, t_h, *free)

            def feed(self, k, t_h, *free):
                self.split(k, t_h, *free)
                self.sq.feed(k, H[:, k, :], t_h)

            def columns(self):
                ps, free = PSW.take()
                t = mean_eps(var[:, :], ps[:, 0:8], self.sq.columns(ps, free))
                PSW.put(ps, t)
                self.t_ic = inv_sqrt(invc[:, :], var[:, :], sd[:, :], t)
                self.dg = diagonals(invc, self.t_ic)

            def spread(self, inv_free=()):
                self.t_inv = spread(self.dg, INV[:, :], free=inv_free)

        def part(norm, w, slot, ks, begin, finish_):
            wh, wl, th, tl = w
            ps, free = slot
            return product(ps, [(wh[:, 128 * k:128 * k + 128], wl[:, 128 * k:128 * k + 128],
                                 UH[:, k, :], UL[:, k, :], th + norm.uh[k] + free, tl + norm.ul[k])
                                for k in ks], begin=begin, finish_=finish_)

        def dense(norm, between={}):
            w, slot = W.get(), PSW.take()
            cuts = sorted({0, *between, 8})
            for k0, k1 in zip(cuts, cuts[1:]):
                if k0 in between:
                    between[k0]()
                t = part(norm, w, slot, range(k0, k1), k0 == 0, k1 == 8)
            return slot[0], t

        def dense_pair(norm, middle=None, ks=range(8)):
            w = [W.get(), W.get()]
            ps = [PSW.take(), PSW.take()]
            for k in (ks[:6], ks[6:]):
                t = [part(norm, w[x], ps[x], k, k[0] == ks[0], k[-1] == ks[-1]) for x in range(2)]
                if middle:
                    middle = middle()
            return [(ps[x][0], t[x]) for x in range(2)]

        N0 = Norm(vec[:, 0:8])
        first = {}

        def start(*ks):
            for x, k in ks:
                if x not in first:
                    first[x] = [W.get(), PSW.take(), None]
                w, slot, _ = first[x]
                first[x][2] = part(N0, w, slot, (k,), k == 0, k == 7)

        N0.split(0, t_h[0])
        W.split()
        start((0, 0))
        N0.split(1, t_h[1])
        W.split()
        start((0, 1), (1, 0), (1, 1))
        N0.split(2, t_h[2])
        W.split()
        start((0, 2), (1, 2), (2, 0), (2, 1), (2, 2))
        for k in range(3, 8):
            N0.split(k, t_h[k])
            N0.sq.feed(k - 3, H[:, k - 3, :], t_h[k - 3], q=dve if k % 2 else pool)
            if k < 6:
                start(*[(x, k) for x in range(3)])
        for k in range(5, 8):
            N0.sq.feed(k, H[:, k, :], t_h[k], q=dve if k % 2 else pool)
        start((0, 6), (0, 7))
        W.done(first[0][2])
        N0.columns()
        start((1, 6), (1, 7))
        N0.spread()
        W.done(first[1][2])
        start((2, 6), (2, 7))
        W.done(first[2][2])

        memo = {"c": [], "xp": [dve.do(lambda e: e.memset(XP[:, 0:16], 0.0))]}
        t_P = [None] * 4
        t_Pfree = [[] for _ in range(4)]

        def pooled(g, i, ps, t):
            w = 2 << g
            t = dve.do(lambda e: e.tensor_tensor(XP[:, 16:1040], ps[:, :], INV[:, :], ALU.mult),
                       t, N0.t_inv, *memo["xp"])
            PSW.put(ps, t)
            src, d = XP, 1
            bufs = []
            while d < w:
                dst, free = TMP.take()
                lo = 2 * d - 1
                t = dve.do(lambda e, dst=dst, src=src, lo=lo, d=d: e.tensor_tensor(
                    dst[:, lo:1040], src[:, lo:1040], src[:, lo - d:1040 - d], ALU.add), t, *free)
                if src is not XP:
                    TMP.put(src, t)
                src, d = dst, 2 * d
            pf, free = TMP.take()
            t1 = dve.do(lambda e: e.scalar_tensor_tensor(
                pf[:, 16:1040], src[:, 16:1040], 1.0 / w, XP[:, 16:1040],
                op0=ALU.mult, op1=ALU.subtract), t, *free)
            t2 = dve.do(lambda e: e.tensor_tensor(EDGE[:, 0:w], src[:, 16:16 + w], vec[:, VC:VC + w],
                                                  ALU.mult), t, t_const, *memo['c'])
            t = dve.do(lambda e: e.tensor_tensor(pf[:, 16:16 + w - 1], EDGE[:, 0:w - 1],
                                                 XP[:, 16:16 + w - 1], ALU.subtract), t1, t2)
            memo["xp"] = memo["c"] = [t]
            TMP.put(src, t)
            th, tl = split(pf[:, 16:1040], PH[i][:, :], PL[i][:, :], t, *t_Pfree[i])
            TMP.put(pf, th, tl)
            t_P[i] = (th, tl)

        VC = 8
        Yslots = Slots([0, 1])
        ys = []

        def x_tile(g, i):
            ps, t = dense(N0)
            pooled(g, i, ps, t)
            W.done(t)

        def z_tile(g, i):
            ps, t = dense(N0)
            z, free = TMP.take()
            tz = mult(z[:, 0:S], ps[:, :], INV[:, :], t, N0.t_inv, *free)
            PSW.put(ps, tz)
            tz = act.do(lambda e: e.activation(z[:, 0:S], z[:, 0:S], ACT.Silu), tz)
            W.done(t)
            return z, tz

        def g_tile(g, i, z, tz, w):
            wh, wl, th, tl = w
            ps, free = PSW.take()
            o = 512 * (i % 2)
            t = product(ps, [(wh[:, o + 128 * k:o + 128 * k + 128], wl[:, o + 128 * k:o + 128 * k + 128],
                              PH[k][:, :], PL[k][:, :], th + [t_P[k][0]] + free, tl + [t_P[k][1]])
                             for k in range(4)])
            y, free = TMP.take()
            sc = vec[:, VS + 4 * g + i:VS + 4 * g + i + 1]
            ty = dve.do(lambda e: e.scalar_tensor_tensor(y[:, 0:S], ps[:, :], sc, z[:, 0:S],
                                                         op0=ALU.mult, op1=ALU.mult), t, tz, t_const, *free)
            PSW.put(ps, ty)
            TMP.put(z, ty)
            b, free = Yslots.take()
            t1, t2 = split(y[:, 0:S], YH[b][:, :], YL[b][:, :], ty, *free)
            TMP.put(y, t1, t2)
            ys.append((b, [t1], [t2]))
            return t

        VS = 24

        def out_tiles(parts, m0, m1, last=None):
            n = len(parts)
            wh, wl, th, tl = W.get()
            for m in range(m0, m1):
                ps, free = PSW.take()
                o = 128 * n * (m - m0)
                t = product(ps, [(wh[:, o + 128 * k:o + 128 * k + 128], wl[:, o + 128 * k:o + 128 * k + 128],
                                  ah, al, th + ta + free, tl + tb)
                                 for k, (ah, al, ta, tb) in enumerate(parts)])
                t_h[m] = dve.do(lambda e, m=m, ps=ps: e.tensor_tensor(
                    H[:, m, :], H[:, m, :], ps[:, :], ALU.add), t, t_h[m])
                PSW.put(ps, t_h[m])
                if last and m > 0:
                    last(m - 1)
            W.done(t)
            if last and m1 == KT:
                last(m1 - 1)
            return t

        def pool_out(last=None):
            parts = [(YH[b][:, :], YL[b][:, :], a, c) for b, a, c in ys]
            out_tiles(parts, 0, 4, last)
            t = out_tiles(parts, 4, 8, last)
            for b, _, _ in ys:
                Yslots.put(b, t)
            ys.clear()

        for x in range(3):
            pooled(0, x, first[x][1][0], first[x][2])
        for g in range(4):
            for i in range(3 if g == 0 else 1, 4):
                x_tile(g, i)
            for pair in range(2):
                za = z_tile(g, 2 * pair)
                if pair:
                    pool_out()
                zb = z_tile(g, 2 * pair + 1)
                t_u = W.use[-1]
                t_inv_old = zb[1]
                w = W.get()
                g_tile(g, 2 * pair, *za, w)
                t = g_tile(g, 2 * pair + 1, *zb, w)
                if pair:
                    for i in range(4):
                        t_Pfree[i] = [t]
                W.done(t)
            if g < 3:
                x_tile(g + 1, 0)
                pool_out()
            else:
                N1 = Norm(vec[:, 40:48])
                pool_out(lambda m: N1.feed(m, t_h[m], t_u))

        QKD = nc.dram_tensor("qk_split", [2, 2, 1024, S], F32).ap()
        VD = nc.dram_tensor("v_split", [2, 16, 128, 8, 128], F32).ap()
        ZD = nc.dram_tensor("z_gate", [16, 128, S], F32).ap()
        QS = Slots([(at(WORK + 8 * i, [S], F32R), at(WORK + 8 * i + 4, [S], F32R),
                     sem(f"s_qs{i}"), sem(f"s_ql{i}")) for i in range(2)], t_Pfree[0])
        VS_ = Slots([(at(WORK + 16 + 4 * i, [512], F32R), at(WORK + 18 + 4 * i, [512], F32R),
                      sem(f"s_vs{i}"), sem(f"s_vl{i}")) for i in range(8)], [(pe.sem, pe.count)])
        s_zd = [sem(f"s_zd{i}") for i in range(4)]
        t_qk, t_v, t_z = {}, {}, {}

        def qk_tile(kind, i, ps, t):
            f, free = TMP.take()
            if kind == 0:
                te = dve.do(lambda e: e.scalar_tensor_tensor(
                    f[:, 0:S], ps[:, :], 0.125, INV[:, :], op0=ALU.mult, op1=ALU.mult), t, N.t_inv, *free)
            else:
                te = mult(f[:, 0:S], ps[:, :], INV[:, :], t, N.t_inv, *free)
            PSW.put(ps, te)
            slot, free = QS.take()
            hi, lo, sh, sl = slot
            th, tl = split(f[:, 0:S], hi[:, :], lo[:, :], te, *free)
            TMP.put(f, th, tl)
            a = sp.dma(QKD[kind, 0, 128 * i:128 * i + 128, :], hi[:, :], sh, th)
            b = sp.dma(QKD[kind, 1, 128 * i:128 * i + 128, :], lo[:, :], sl, tl)
            QS.put(slot, a, b)
            t_qk[kind, i] = (a, b)

        N = N1
        pair = dense_pair(N)
        for x in range(2):
            W.done(pair[x][1])
        third = dense(N, {4: N.columns, 7: lambda: N.spread([t_inv_old])})
        W.done(third[1])
        for x in range(2):
            qk_tile(x, 0, *pair[x])
        for i in range(2, 16):
            ps, t = third if i == 2 else dense(N)
            qk_tile(i % 2, i // 2, ps, t)
            if i > 2:
                W.done(t)

        slots8 = [PSW.take() for _ in range(4)]
        vfree = [f for _, f in slots8 for _ in range(2)]
        for g in range(4):
            for k in range(8):
                if k % 2 == 0:
                    wh, wl, th, tl = W.get()
                r = slice(512 * (k % 2), 512 * (k % 2) + 512)
                ends = []
                for j in range(8):
                    ps, free = slots8[j // 2][0], vfree[j]
                    o = slice(512 * (j % 2), 512 * (j % 2) + 512)
                    js = slice(128 * j, 128 * j + 128)
                    for i, (l, m) in enumerate(((UH, wh), (UL, wh), (UH, wl))):
                        t = pe.do(lambda e, ps=ps, o=o, l=l, m=m, js=js, k=k, r=r, i=i: e.matmul(
                            ps[:, o], l[:, k, js], m[:, r], start=k == 0 and i == 0,
                            stop=k == 7 and i == 2), *(th + free + N.uh[k] if i == 0 else tl + N.ul[k]),
                            mark=i == 2 and (k == 7 or j == 7))
                    ends.append(t)
                if k % 2 == 1 and k < 7:
                    W.done(t)
            for j in range(8):
                ps = slots8[j // 2][0]
                o = slice(512 * (j % 2), 512 * (j % 2) + 512)
                slot, free = VS_.take()
                hi, lo, sh, sl = slot
                th = act.do(lambda e, ps=ps, o=o, j=j, hi=hi: e.activation(
                    hi[:, :], ps[:, o], ACT.Copy, scale=invc[:, j:j + 1]), ends[j], N.t_ic, *free)
                tl = dve.do(lambda e, ps=ps, o=o, j=j, hi=hi, lo=lo: e.scalar_tensor_tensor(
                    lo[:, :], ps[:, o], invc[:, j:j + 1], hi[:, :].bitcast(F32),
                    op0=ALU.mult, op1=ALU.subtract), th, *free)
                vfree[j] = [th, tl]
                hs = slice(4 * g, 4 * g + 4)
                a = sp.dma(VD[0, hs, :, j, :].rearrange("h p c -> p h c"),
                           hi[:, :].rearrange("p (h c) -> p h c", h=4), sh, th)
                b = sp.dma(VD[1, hs, :, j, :].rearrange("h p c -> p h c"),
                           lo[:, :].rearrange("p (h c) -> p h c", h=4), sl, tl)
                VS_.put(slot, a, b)
                t_v[g, j] = (a, b)
            W.done(t)
        for i, (ps, _) in enumerate(slots8):
            PSW.put(ps, *vfree[2 * i], *vfree[2 * i + 1])

        def gate(i, ps, t):
            z, free = TMP.take()
            tz = mult(z[:, 0:S], ps[:, :], INV[:, :], t, N.t_inv, *free)
            PSW.put(ps, tz)
            tz = act.do(lambda e: e.activation(z[:, 0:S], z[:, 0:S], ACT.Silu), tz)
            W.done(t)
            t_z[i] = sp.dma(ZD[i], z[:, 0:S], s_zd[tmps.index(z)], tz)
            TMP.put(z, t_z[i])
            t_gates.extend((t_z[i], tz))

        t_gates = []
        NZ = 14
        t_idr = pool.do(lambda e: e.tensor_copy(identr[:, :], ident[:, :]), t_ident)
        s_mask = sem("s_mask")
        mk, f = TMP.take()
        t_mask = sp.dma(mk[:, 0:128], A["mask"], s_mask, *f)
        t_mask = pool.do(lambda e: e.tensor_copy(maskr[:, :], mk[:, 0:128]), t_mask)
        TMP.put(mk, t_mask)

        q_free = [tok for ring in (QS, VS_) for _, f in ring.line for tok in f]
        t_u1 = []

        QKR, VR, ZR = Slots([]), Slots([]), Slots([])
        for i, (kb, free) in enumerate(((139, q_free), (32, t_u1))):
            QKR.line.append((([at(kb + 4 * j, [S], F32R) for j in range(3)],
                              [sem(f"s_qkr{i}_{j}") for j in range(3)]), free))
            VR.line.append((([at(kb + 12 + 4 * j, [8, 128], F32R) for j in range(2)], sem(f"s_vr{i}")), free))
            ZR.line.append(((at(kb + 20, [S]), sem(f"s_zr{i}")), free))
        qk_of, v_of, z_of = {}, {}, {}

        def load_qk(h):
            (bufs, sems), free = QKR.take()
            r = slice(64 * h, 64 * h + 64)
            toks = []
            for j, (kind, hi, lo) in enumerate(((1, 0, 1), (0, 0, 0), (0, 1, 1))):
                for x, part in ((0, hi), (1, lo)):
                    t = sp.dma(bufs[j][64 * x:64 * x + 64, :], QKD[kind, part, r, :], sems[j],
                               *free, t_qk[kind, h // 2][part])
                toks.append(t)
            qk_of[h] = bufs, sems, toks

        def load_v(h):
            ((vh, vl), s_v), free = VR.take()
            toks = [tok for j in range(8) for tok in t_v[h // 4, j]]
            sp.dma(vh[:, :, :], VD[0, h], s_v, *free, *toks)
            v_of[h] = vh, vl, s_v, sp.dma(vl[:, :, :], VD[1, h], s_v, *free, *toks)
            (z, s_z), free = ZR.take()
            z_of[h] = z, s_z, sp.dma(z[:, :], ZD[h], s_z, *free, t_z[h])

        load_qk(0)
        for i in range(NZ):
            gate(i, *dense(N))
        load_v(0)
        for _ in range(4):
            t, f = TMP.take()
            if t in tmps[:2]:
                q_free += f
            else:
                TMP.put(t, *f)

        banks = [PSW.take() for _ in range(3)]
        half = [((b, n), f) for b, f in banks for n in range(2)]

        def bank(b):
            return b[0][:, 512 * b[1]:512 * b[1] + 512]

        LG, OA = Slots([]), Slots([])
        TP, WB = LG, OA
        for i, (b, f) in enumerate(half):
            (LG if i < 4 else OA).put(b, *f)

        def ring(kbs, make):
            r = Slots([])
            for kb in kbs:
                r.line.append((make(kb), t_u1 if kb < 100 else q_free))
            return r

        OM = ring((187, 191, 195), lambda kb: at(kb, [S]))
        BT = ring((163, 167, 171, 175, 179, 183), lambda kb: at(kb, [S]))
        ATS = ring((56, 60, 84, 88, 92), lambda kb: (at(kb, [512], F32R), at(kb + 2, [512], F32R)))
        YF = ring((64,), lambda kb: at(kb, [S]))
        YS = ring((68, 76), lambda kb: (at(kb, [S], F32R), at(kb + 4, [S], F32R)))
        YS.line.append(((at(199.1875, [S], F32R), at(203.1875, [S], F32R)), t_gates))

        A_of = {}
        ON_DVE = (5,)

        def logits(h, tt):
            n = 128 * (tt + 1)
            qs = slice(128 * tt, 128 * tt + 128)
            st = {"sig": []}

            def unit(c0):
                if c0 == 0:
                    st["om"], st["omf"] = OM.take()
                    st["bt"], st["btf"] = BT.take()
                (kx, q1, q2), sems, (tk, t1, t2) = qk_of[h]
                c1 = min(c0 + 512, n)
                lg, f = LG.take()
                ps = bank(lg)
                diag = c1 == n
                pe.do(lambda e: e.matmul(ps[:, 0:c1 - c0], q1[:, qs], kx[:, c0:c1],
                                         start=True, stop=False), tk, t1, *f, mark=False)
                t = pe.do(lambda e: e.matmul(ps[:, 0:c1 - c0], q2[:, qs], kx[:, c0:c1],
                                             start=False, stop=not diag), t2, mark=not diag)
                if diag:
                    t = pe.do(lambda e: e.matmul(ps[:, c1 - c0 - 128:c1 - c0], identr[:, :],
                                                 maskr[:, :], start=False, stop=True), t_idr, t_mask)
                    if tt == 7:
                        QKR.put(qk_of[h][:2], t)
                        if h < 14:
                            load_qk(h + 2)
                t1 = act.do(lambda e: e.activation(st["om"][:, c0:c1], ps[:, 0:c1 - c0], ACT.Sigmoid,
                                                   scale=-1.0), t, *st["omf"])
                t2 = act.do(lambda e: e.activation(st["bt"][:, c0:c1], ps[:, 0:c1 - c0], ACT.Sigmoid),
                            t, *st["btf"])
                LG.put(lg, t1, t2)
                st["sig"] += [t1, t2]

            def weights():
                om, bt = st["om"], st["bt"]
                rev = om[:, n - 1::-1]
                t = dve.do(lambda e: e.tensor_tensor_scan(rev, rev, rev, 1.0, ALU.mult, ALU.bypass),
                           *st["sig"])
                t = mult(bt[:, 0:n - 1], bt[:, 0:n - 1], om[:, 1:n], t, *st["sig"],
                         q=dve if tt in ON_DVE else pool)
                OM.put(om, t)
                A_of[h, tt] = bt, t

            atoms = [(lambda c0=c0: unit(c0)) for c0 in range(0, n, 512)]
            return [(a, weights if i == len(atoms) - 1 else None) for i, a in enumerate(atoms)]

        def turned(h, p, m):
            tp, f = TP.take()
            ps = bank(tp)
            blocks = [(0, 2 * m, 0), (1, 2 * m, 128)]
            blocks += [(1, 2 * m + 1, 256)] if m == p else [(0, 2 * m + 1, 256), (1, 2 * m + 1, 384)]
            for x, j, o in blocks:
                bt, ta = A_of[h, 2 * p + x]
                t = pe.do(lambda e: e.transpose(ps[:, o:o + 128], bt[:, 128 * j:128 * j + 128],
                                                ident[:, :]), ta, *f, mark=o == blocks[-1][2])
            n = 128 * len(blocks)
            if m == p:
                for x in range(2):
                    BT.put(A_of.pop((h, 2 * p + x))[0], t)
            (hi, lo), f = ATS.take()
            th = act.do(lambda e: e.activation(hi[:, 0:n], ps[:, 0:n], ACT.Copy), t, *f)
            tl = dve.do(lambda e: e.tensor_tensor(lo[:, 0:n], ps[:, 0:n], hi[:, 0:n].bitcast(F32),
                                                  ALU.subtract), th, *f)
            TP.put(tp, tl)
            return hi, lo, th, tl

        o_of = {}

        def times(h, p, m, at_, low):
            hi, lo, th, tl = at_
            if m == 0 and not low:
                o_of[h, p] = OA.take()
            bk, free = o_of[h, p]
            ps = bank(bk)
            vh, vl, s_v, tv = v_of[h]
            for i in range(2):
                j = 2 * m + i
                c = slice(128, 256) if m == p and i else slice(0, 256)
                src = slice(256, 384) if m == p and i else slice(256 * i, 256 * i + 256)
                for x, (v, a) in enumerate(((vh, lo),) if low else ((vh, hi), (vl, hi))):
                    t = pe.do(lambda e: e.matmul(ps[:, c], v[:, j, :], a[:, src],
                                                 start=m == 0 and i == 0 and x == 0 and not low,
                                                 stop=m == p and i == 1 and low),
                              tv, tl if low else th, *free, mark=i == 1 and (low or x == 1))
            if not low:
                return
            ATS.put((hi, lo), t)
            if m == p:
                if p == 0:
                    yf_now[h] = YF.take()
                yf, f = yf_now[h]
                z, s_z, tz = z_of[h]
                c = slice(256 * p, 256 * p + 256)
                ty = mult(yf[:, c], ps[:, 0:256], z[:, c], t, tz, *f)
                OA.put(bk, ty)
                if p == 3:
                    if h == 14:
                        YS.line.insert(0, ((at(151, [S], F32R), at(155, [S], F32R)), [t]))
                    y, f = YS.take()
                    t1, t2 = split(yf[:, :], y[0][:, :], y[1][:, :], ty, *f, q=pool)
                    YF.put(yf, t1, t2)
                    VR.put(((vh, vl), s_v), t)
                    ZR.put((z, s_z), ty)
                    if h < 14:
                        load_v(h + 2)
                    y_now.append((y, [t1], [t2]))

        yf_now, y_now = {}, []

        filler = []

        def z_parts(i):
            box = {}

            def part(c):
                if c == 0:
                    box["w"], box["ps"] = W.get(), PSW.take()
                wh, wl, th, tl = box["w"]
                ps, free = box["ps"]
                t = product(ps, [(wh[:, 128 * k:128 * k + 128], wl[:, 128 * k:128 * k + 128],
                                  UH[:, k, :], UL[:, k, :], th + free, tl)
                                 for k in (2 * c, 2 * c + 1)], begin=c == 0, finish_=c == 3)
                if c == 3:
                    gate(i, ps, t)
                    if i == 15:
                        t_u1.append(t)
                        take_wbanks()
            return [lambda c=c: part(c) for c in range(4)]

        def take_wbanks():
            b, f = PSW.take()
            for n in range(2):
                WB.put((b, n), *f)

        def out_half(parts, m, n, first, last, t_hold, m0):
            if first:
                w_now[0] = W.get()
            wh, wl, th, tl = w_now[0]
            wb, f = WB.take()
            ps = bank(wb)
            c = slice(512 * n, 512 * n + 512)
            for k, (ah, al, ta, tb) in enumerate(parts):
                o = 256 * (m - m0) + 128 * k
                for i, (l, r) in enumerate(((wh, ah), (wl, ah), (wh, al))):
                    end = k == 1 and i == 2
                    t = pe.do(lambda e, l=l, r=r, o=o, s=k == 0 and i == 0, end=end: e.matmul(
                        ps[:, :], l[:, o:o + 128], r[:, c], start=s, stop=end),
                        *(th + ta + f if i == 0 else tl + tb), mark=end)
            t_h[m] = dve.do(lambda e: e.tensor_tensor(H[:, m, c], H[:, m, c], ps[:, :], ALU.add),
                            t, t_h[m])
            WB.put(wb, t_h[m])
            if last:
                W.done(t)
            t_hold[0] = t

        w_now = [None]

        def out_atoms():
            pair = y_now[:2]
            del y_now[:2]
            parts = [(y[0], y[1], a, c) for y, a, c in pair]
            hold = [None]

            def atom(m, n):
                out_half(parts, m, n, m % 4 == 0 and n == 0, m % 4 == 3 and n == 1, hold, m // 4 * 4)
                if m == 7 and n == 1:
                    for y, _, _ in pair:
                        YS.put(y, hold[0])
            return [lambda m=m, n=n: atom(m, n) for m in range(8) for n in range(2)]

        W.q = pool
        steps = [(h, p) for h in range(16) for p in range(4)]
        soon = []

        def issue(fn, after=None):
            fn()
            for x in soon:
                x[0] -= 1
            while soon and soon[0][0] <= 0:
                soon.pop(0)[1]()
            if after:
                soon.append([1, after])

        def pair_logits(h, p):
            return [a for tt in (2 * p, 2 * p + 1) for a in logits(h, tt)]

        for i in (14, 15):
            for a in pair_logits(0, i - 14):
                issue(*a)
            for fn in z_parts(i):
                issue(fn)
        load_qk(1)
        load_v(1)
        HIGH, LOW = 1, 2
        FILL = (5, 3, 2, 0)
        line = []

        def unit(h, p, m):
            line.append((h, p, m, turned(h, p, m)))
            if len(line) > LOW:
                times(*line.pop(0), True)
            if len(line) > HIGH:
                times(*line[-1 - HIGH], False)

        for P, (h, p) in enumerate(steps):
            todo = []
            if P < 62:
                q = pair_logits(*steps[P + 2])
                todo += [(0.7 * i / len(q), 0, a) for i, a in enumerate(q)]
            todo += [((m + 0.3) / (p + 1), 1, ((lambda m=m: unit(h, p, m)), None)) for m in range(p + 1)]
            nf = FILL[p]
            fl, filler = filler[:nf], filler[nf:]
            todo += [((i + 0.5) / len(fl), 2, (fn, None)) for i, fn in enumerate(fl)]
            for _, _, a in sorted(todo, key=lambda x: x[:2]):
                issue(*a)
            if len(y_now) == 2 and h < 15:
                filler += out_atoms()
        for i in range(HIGH, 0, -1):
            times(*line[-i], False)
        while line:
            times(*line.pop(0), True)
        for fn in filler:
            fn()

        end = [(q.sem, q.count) for q in (pe, act, dve, pool)]
        PSW = Slots([])
        for ps in psum:
            PSW.put(ps, *[tok for ring in (LG, OA) for (b, _), f in ring.line if b is ps for tok in f])
        TMP = Slots([])
        places = [149.3125 + 4 * i for i in range(7)] + [203.3125]
        tmps = [at(kb, [S]) for kb in places]
        tmps_r = [at(kb, [S], F32R) for kb in places]
        for t in tmps[3:7]:
            TMP.put(t, *end)
        small = iter([at(141.5 + 0.25 * i, [64]) for i in range(15)])
        TI, TS = at(139, [128]), at(139.5, [128])
        wab_h, wab_l = at(140, [128], F32R), at(140.5, [128], F32R)
        gfm = at(141, [8])
        cg = at(141.0625, [112])
        CB = at(145.25, [1040])

        s_g = sem("s_g")
        sp.dma(TI[:, :], A["tri_incl"], s_g, *end)
        sp.dma(TS[:, :], A["tri_strict"], s_g, *end)
        t_cg = sp.dma(cg[:, :], A["gdn_vec"], s_g, *end)
        t_gfm = mult(gfm[:, :], vec[:, 48:56], vec[:, 56:64], t_const, *end)
        t_pad = dve.do(lambda e: e.memset(CB[:, 0:16], 0.0), *end)

        parts = [(y[0], y[1], a, c) for y, a, c in y_now]
        nf2 = at(145.1875, [8])
        t_nf2 = mult(nf2[:, :], vec[:, 48:56], vec[:, 48:56], t_const, *end)
        N2 = Norm(gfm, (nf2, t_nf2))

        def feed2(m):
            N2.feed(m, t_h[m], t_gfm, *end)

        s_ab = sem("s_ab")
        ab, f = TMP.take()
        t = sp.dma(ab[:, 0:128], A["gdn_ab"], s_ab, *f)
        t_wab = split(ab[:, 0:128], wab_h[:, :], wab_l[:, :], t)
        TMP.put(ab, *t_wab)
        HD = nc.dram_tensor("h2", [KT, 128, S], F32).ap()
        s_hd = [sem(f"s_hd{m}") for m in range(8)]
        t_hd = [None] * 8

        def feed3(m):
            feed2(m)
            t_hd[m] = sp.dma(HD[m], H[:, m, :], s_hd[m], t_h[m])

        W.q = act
        out_tiles(parts, 0, 4, feed3)
        t = out_tiles(parts, 4, 8, feed3)
        t_last = [t]
        for b in tmps[:3] + tmps[7:]:
            TMP.put(b, t, *end)

        ivf, var2 = next(small), next(small)
        memo = {}

        def two_columns():
            ps, f = PSW.take()
            t = N2.sq.columns(ps, f)
            t2 = N2.sq.columns2(ps[:, 512:520], f)
            ta = mean_eps(var[:, :], ps[:, 0:8], t)
            tb = dve.do(lambda e: e.tensor_scalar(var2[:, 0:8], ps[:, 512:520], 1.0 / D, None, op0=ALU.mult),
                        t2, *end)
            PSW.put(ps, tb, ta)
            t = dve.do(lambda e: e.scalar_tensor_tensor(
                var2[:, 0:8], var[:, :], EPS, var2[:, 0:8], op0=ALU.mult, op1=ALU.add), ta, tb)
            t = inv_sqrt(invc[:, :], var2[:, 0:8], sd[:, :], t)
            memo["i"] = diagonals(invc, t)
            memo["f"] = inv_sqrt(ivf[:, 0:8], var[:, :], sd[:, :], t)

        pair = dense_pair(N2, two_columns)
        W.done(pair[0][1])
        W.done(pair[1][1])
        W.q = pool
        t_f = memo["f"]

        psab, f = PSW.take()
        for k in range(8):
            if k == 2:
                N2.t_inv = spread(memo["i"], INV[:, :], free=t_last)
            for i, (l, r) in enumerate(((wab_h, UH), (wab_l, UH), (wab_h, UL))):
                for n in range(2):
                    t_ab = pe.do(lambda e: e.matmul(
                        psab[0:16, 512 * n:512 * n + 512], l[:, 16 * k:16 * k + 16],
                        r[:, k, 512 * n:512 * n + 512], start=k == 0 and i == 0,
                        stop=k == 7 and i == 2), *t_wab, *f, mark=k == 7 and i == 2)

        KTD, KDD, QTD, QKT, VPD, GTD = (
            nc.dram_tensor(n, [8, 128, 8, 128], F32).ap() for n in ("kt", "kd", "qt", "qkt", "vp", "gt"))
        LTD = nc.dram_tensor("lt", [64, 128, 128], F32).ap()
        UD = nc.dram_tensor("ut", [64, 128, 128], F32).ap()
        TBD = nc.dram_tensor("tb", [128, 32, 32], F32).ap()
        UBD = nc.dram_tensor("ub", [128, 32, 32], F32).ap()
        T64 = nc.dram_tensor("t64", [64, 64, 64], F32).ap()

        s_tmp = {id(t): sem(f"s_gtmp{i}") for i, t in enumerate(tmps)}

        def store(dst, t, *after):
            tok = sp.dma(dst, t[:, :].rearrange("p (b c) -> p b c", b=8), s_tmp[id(t)], *after)
            TMP.put(t, tok, *after)
            return tok

        E = [at(4 * h, [8, 128]) for h in range(8)]

        s_zero = sem("s_zero")
        zt, f = TMP.take()
        tz = pool.do(lambda e: e.memset(zt[:, :], 0.0), *f)
        for i in range(8):
            t_zero = sp.dma(UD[8 * i:8 * i + 8].rearrange("n (x y) c -> (n x) (y c)", x=16), zt[:, :],
                            s_zero, tz)
        for i in range(2):
            t_zero = sp.dma(T64[32 * i:32 * i + 32].rearrange("n (x y) c -> (n x) (y c)", x=4),
                            zt[:, :], s_zero, tz)
        TMP.put(zt, t_zero)

        abT, f = TMP.take()
        t = mult(abT[0:16, :], psab[0:16, :], INV[0:16, :], t_ab, N2.t_inv, *f)
        PSW.put(psab, t)
        psa, f = PSW.take()
        for j in range(8):
            t2 = pe.do(lambda e: e.transpose(psa[:, 16 * j:16 * j + 16], abT[0:16, 128 * j:128 * j + 128],
                                             ident[0:16, 0:16]), t, *f, mark=j == 7)
        TMP.put(abT, t2)
        t_pab = t2
        pab = psa[:, 0:128].rearrange("p (b c) -> p b c", b=8)
        gg, spl, beta, eG, eGLG, eGL, ssk, nk, bc, cneg, ssq = (next(small) for _ in range(11))

        def v3(t):
            return t[:, :].rearrange("p (b c) -> p b c", b=8)

        def row(c):
            return cg[:, c:c + 8].unsqueeze(1).broadcast_to([128, 8, 8])

        eGn = next(small)
        t_be = t_g = t_eg = t_egn = t5 = None

        def small_gates():
            nonlocal t_be, t_g, t5
            ta = dve.do(lambda e: e.tensor_tensor(v3(gg), pab[:, :, 0:8], row(104), ALU.add),
                        t_pab, t_cg, *end)
            tb = dve.do(lambda e: e.tensor_scalar(v3(beta), pab[:, :, 8:16], 1.0, None, op0=ALU.mult),
                        t_pab, *end)
            PSW.put(psa, ta, tb)
            t_be = act.do(lambda e: e.activation(beta[:, :], beta[:, :], ACT.Sigmoid), tb)
            t1 = act.do(lambda e: e.activation(spl[:, :], gg[:, :], ACT.Abs), ta)
            t1 = act.do(lambda e: e.activation(spl[:, :], spl[:, :], ACT.Exp, scale=-1.0), t1)
            te = act.do(lambda e: e.activation(cneg[:, 0:8], cg[:, 96:104], ACT.Exp), t_cg, *end)
            t2 = dve.do(lambda e: e.tensor_scalar(nk[:, :], spl[:, :], 1.0, None, op0=ALU.add), t1, *end)
            t3 = act.do(lambda e: e.activation(eG[:, :], nk[:, :], ACT.Ln), t2)
            t4 = dve.do(lambda e: e.scalar_tensor_tensor(spl[:, :], nk[:, :], -1.0, spl[:, :],
                                                         op0=ALU.add, op1=ALU.subtract), t2)
            t5 = dve.do(lambda e: e.reciprocal(nk[:, :], nk[:, :]), t4, t3)
            t5 = mult(spl[:, :], spl[:, :], nk[:, :], t5)
            t5 = dve.do(lambda e: e.tensor_tensor(spl[:, :], eG[:, :], spl[:, :], ALU.subtract), t5, t3)
            t5 = dve.do(lambda e: e.scalar_tensor_tensor(spl[:, :], gg[:, :], 0.0, spl[:, :],
                                                         op0=ALU.max, op1=ALU.add), t5)
            t_g = dve.do(lambda e: e.scalar_tensor_tensor(
                v3(gg), v3(spl), -1.0, cneg[:, 0:8].unsqueeze(1).broadcast_to([128, 8, 8]),
                op0=ALU.mult, op1=ALU.mult), t5, te)

        def small_decays():
            nonlocal t_eg, t_egn
            psg, f = PSW.take()
            for i, (l, tl) in enumerate(((TI, t_cg), (TS, t_cg), (ones, t_ones))):
                t = pe.do(lambda e: e.matmul(psg[:, 64 * i:64 * i + 64], l[:, :], gg[:, :],
                                             start=True, stop=True), t_g, tl, *f)
            for i, d in enumerate((eG, eGLG, eGL)):
                t_eg = act.do(lambda e: e.activation(d[:, :], psg[:, 64 * i:64 * i + 64], ACT.Exp), t, t5)
            PSW.put(psg, t_eg)
            t_egn = dve.do(lambda e: e.tensor_scalar(eGn[:, :], eG[:, :], -1.0, None, op0=ALU.mult),
                           t_eg, *end)

        t_E = {}

        TSR, gh, gl = at(140, [128], F32R), at(140.5, [64], F32R), at(140.75, [64], F32R)
        gts = {}

        def split_g():
            free = [t_ab]
            box["tsr"] = pool.do(lambda e: e.tensor_copy(TSR[:, :], TS[:, :]), t_cg, *free)
            box["gh"] = split(gg[:, :], gh[:, :], gl[:, :], t_g, *free, q=pool, ql=pool)

        def start_decay(h):
            gts[h] = []
            for g, tg in zip((gh, gl), box["gh"]):
                gt, f = TMP.take()
                gr = tmps_r[tmps.index(gt)]
                gts[h].append((gt, gr, pool.do(lambda e: e.tensor_tensor(
                    gr[:, :].rearrange("p (b c) -> p b c", b=8),
                    TI[:, :].unsqueeze(1).broadcast_to([128, 8, 128]),
                    v3(g.bitcast(F32))[:, :, h:h + 1].broadcast_to([128, 8, 128]), ALU.mult), tg, t_cg, *f)))

        def decay(h):
            ps, f = PSW.take()
            for x, (gt, gr, t) in enumerate(gts.pop(h)):
                for n in range(2):
                    t2 = pe.do(lambda e: e.matmul(
                        ps[:, 512 * n:512 * n + 512], TSR[:, :],
                        gr[:, 512 * n:512 * n + 512], start=x == 0, stop=x == 1),
                        t, box["tsr"], *f, mark=n == 1)
                TMP.put(gt, t2)
            t_E[h] = act.do(lambda e: e.activation(
                E[h][:, :, :].rearrange("p b c -> p (b c)"), ps[:, :], ACT.Exp), t2, t_hd[h], N2.ul[h][0],
                N2.sq.t, N2.sq.t2)
            PSW.put(ps, t_E[h])

        cb = {"free": [t_pad]}

        def conv_in(c, ps, t):
            t = dve.do(lambda e: e.tensor_tensor(CB[:, 16:1040], ps[:, :], INV[:, :], ALU.mult),
                       t, N2.t_inv, *cb["free"])
            PSW.put(ps, t)
            a, f = TMP.take()
            return a, act.do(lambda e: e.activation(a[:, :], CB[:, 16:1040], ACT.Copy,
                                                    scale=cg[:, 4 * c + 3:4 * c + 4]), t, t_cg, *f)

        def conv_silu(c, a, t):
            for i in (2, 1, 0):
                t = dve.do(lambda e: e.scalar_tensor_tensor(
                    a[:, :], CB[:, 13 + i:1037 + i], cg[:, 4 * c + i:4 * c + i + 1], a[:, :],
                    op0=ALU.mult, op1=ALU.add), t)
            cb["free"] = [t]
            return a, act.do(lambda e: e.activation(a[:, :], a[:, :], ACT.Silu), t)

        def natural(a, t):
            ps, f = PSW.take()
            for j in range(8):
                t2 = pe.do(lambda e: e.transpose(ps[:, 128 * j:128 * j + 128],
                                                 a[:, 128 * j:128 * j + 128], ident[:, :]),
                           t, t_ident, *f, mark=j == 7)
            return ps, t2

        def blocks(l, r, *after):
            ps, f = PSW.take()
            for j in range(8):
                t = pe.do(lambda e: e.matmul(ps[:, 128 * j:128 * j + 128], l[:, 128 * j:128 * j + 128],
                                             r[:, 128 * j:128 * j + 128], start=True, stop=True),
                          *after, *f, mark=j == 7)
            return ps, t

        def b3(x):
            return x.rearrange("p (b c) -> p b c", b=8)

        def per_row(col, h):
            return v3(col)[:, :, h:h + 1].broadcast_to([128, 8, 128])

        def square_rows(ps, t, dst, h):
            sq, f = TMP.take()
            t1 = act.do(lambda e: e.activation(sq[:, :], ps[:, :], ACT.Square), t, *f)
            t2 = dve.do(lambda e: e.tensor_reduce(v3(dst)[:, :, h], b3(sq[:, :]), AX.X, ALU.add), t1)
            TMP.put(sq, t2)
            return t1, t2

        t_kt, t_kd, t_lt, t_b = [], [], [], []

        def k_head(h, a, ta):
            psn, t = natural(a, ta)
            t_sq, t_ss = square_rows(psn, t, ssk, h)
            kd, f = TMP.take()
            t1 = dve.do(lambda e: e.tensor_tensor(b3(kd[:, :]), b3(psn[:, :]), per_row(eGLG, h),
                                                  ALU.mult), t, t_eg, t_sq, *f)
            PSW.put(psn, t1)
            t_kd.append(store(KDD[:, :, h, :].rearrange("b p c -> p b c"), kd, t1))
            psk, t = blocks(a, a, ta)
            c = [v3(x)[:, :, h] for x in (ssk, bc, cneg, beta)]
            t1 = dve.do(lambda e: e.tensor_scalar(c[0], c[0], EPS, None, op0=ALU.add), t_ss)
            t1 = dve.do(lambda e: e.reciprocal(c[1], c[0]), t1, *end)
            t1 = mult(c[1], c[1], c[3], t1, t_be)
            t_b.append(t1)
            t1 = dve.do(lambda e: e.tensor_scalar(c[2], c[1], -1.0, None, op0=ALU.mult), t1, t_g)
            lt, f = TMP.take()
            t2 = dve.do(lambda e: e.tensor_tensor(b3(lt[:, :]), b3(psk[:, :]), E[h][:, :, :], ALU.mult),
                        t, t_E[h], *f)
            PSW.put(psk, t2)
            t2 = pool.do(lambda e: e.tensor_tensor(b3(lt[:, :]), b3(lt[:, :]), per_row(cneg, h),
                                                   ALU.mult), t2, t1)
            t_lt.append(store(LTD[h::8].rearrange("b p c -> p b c"), lt, t2))
            t_kt.append(store(KTD[:, :, h, :].rearrange("b p c -> p b c"), a, ta, t))

        tiles = {0: pair[0], 1: pair[1]}
        ready = {}
        box = {}

        def advance(n, c, behind):
            if n != 1:
                x = conv_in(c, *tiles.pop(n))
            if n == 0:
                small_gates()
                split_g()
                start_decay(0)
                ready[0] = conv_silu(c, *x)
                ready[1] = conv_silu(c + 1, *conv_in(c + 1, *tiles.pop(1)))
            if n > 9:
                substitute_until((n - 9) / 8)
            for m in range(max(n + 1, 2), max(n + 1, 3) + 1):
                if m not in tiles:
                    tiles[m] = dense(N2)
                    W.done(tiles[m][1])
            for fn in behind:
                fn()
            if n > 1:
                ready[n] = conv_silu(c, *x)

        def norm_k():
            tn = act.do(lambda e: e.activation(nk[:, :], ssk[:, :], ACT.Sqrt), t_b[7], t5)
            t = dve.do(lambda e: e.reciprocal(spl[:, :], nk[:, :]), tn)
            t = mult(spl[:, :], spl[:, :], ssk[:, :], t)
            t = dve.do(lambda e: e.tensor_tensor(nk[:, :], nk[:, :], spl[:, :], ALU.add), t)
            box["nk"] = dve.do(lambda e: e.tensor_scalar(nk[:, :], nk[:, :], 0.5, None, op0=ALU.mult), t)

        t_qt, t_qk = [], []

        kts = {}

        def fetch_kt(h):
            kt, f = TMP.take()
            kts[h] = kt, sp.dma(kt[:, :].rearrange("p (b c) -> p b c", b=8),
                                KTD[:, :, h, :].rearrange("b p c -> p b c"), s_ktin[id(kt)], t_kt[h], *f)

        def q_head(h, a, ta):
            kt, t_k = kts.pop(h)
            psn, t = natural(a, ta)
            PSW.put(psn, square_rows(psn, t, ssq, h)[0])
            psk, t = blocks(kt, a, ta, t_k)
            TMP.put(kt, t)
            qk, f = TMP.take()
            t2 = dve.do(lambda e: e.tensor_tensor(b3(qk[:, :]), b3(psk[:, :]), E[h][:, :, :], ALU.mult),
                        t, t_E[h], *f)
            PSW.put(psk, t2)
            t2 = pool.do(lambda e: e.tensor_tensor(
                b3(qk[:, :]), b3(qk[:, :]), TI[:, :].unsqueeze(1).broadcast_to([128, 8, 128]),
                ALU.mult), t2)
            t_qk.append(store(QKT[:, :, h, :].rearrange("b p c -> p b c"), qk, t2))
            t_qt.append(store(QTD[:, :, h, :].rearrange("b p c -> p b c"), a, ta, t))

        s_ktin = {id(t): sem(f"s_ktin{i}") for i, t in enumerate(tmps)}

        t_vp = []

        def v_head(h, a, t):
            psn, t = natural(a, t)
            TMP.put(a, t)
            vp, f = TMP.take()
            t1 = dve.do(lambda e: e.tensor_tensor(b3(vp[:, :]), b3(psn[:, :]), per_row(nk, h),
                                                  ALU.mult), t, box["nk"], *f)
            PSW.put(psn, t1)
            t_vp.append(store(VPD[:, :, h, :].rearrange("b p c -> p b c"), vp, t1))

        NB = at(177.3125, [2, 32, 32])
        UB = at(185.3125, [2, 32, 32])
        PB = at(193.3125, [2048])

        def start_substitution():
            free = [(q.sem, q.count) for q in (pe, act, dve, pool)]
            s_nb = sem("s_nb")
            for hf in range(2):
                for k in range(2):
                    o = 64 * hf + 32 * k
                    box["nb"] = sp.dma(NB[64 * hf:64 * hf + 64, k, :, :], LTD[:, o:o + 32, o:o + 32],
                                       s_nb, *free, *t_lt)
            t = dve.do(lambda e: e.memset(UB[:, :, :, :], 0.0), *free)
            box["u"] = box["p"] = dve.do(lambda e: e.memset(
                UB[:, :, :, :].rearrange("p k a b -> p k (a b)")[:, :, ::33], 1.0), t)

        def substitute(j):
            n = 31 - j
            pb = PB[:, 0:2 * n * n].rearrange("p (k c i) -> p k c i", k=2, c=n)
            box["p"] = dve.do(lambda e: e.tensor_tensor(
                pb, UB[:, :, j + 1:32, j + 1:32].rearrange("p k i c -> p k c i"),
                NB[:, :, j:j + 1, j + 1:32].broadcast_to([128, 2, n, n]), ALU.mult),
                box["nb"], box["u"], box["p"])
            box["u"] = box["p"] = dve.do(lambda e: e.tensor_reduce(
                UB[:, :, j, j + 1:32], pb, AX.X, ALU.add), box["p"])

        q_todo = [lambda j=j: substitute(j) for j in range(30, -1, -1)]
        cost = [(31 - j) ** 2 + 100 for j in range(30, -1, -1)]

        total = sum(cost)

        def substitute_until(share):
            while q_todo and sum(cost) > total * (1 - share):
                cost.pop(0)
                q_todo.pop(0)()

        t_tb = t_ub = t_tbd = t_ud = t_t64 = t_ob = tl = tra = trb = free = None
        TB = at(193.3125, [2, 32, 32])
        LB = at(0, [32, 128])
        OB = at(16, [32, 128])
        RA = at(177.3125, [32, 32])
        RB = at(181.3125, [32, 32])

        def start_joins():
            nonlocal t_tb, t_ub, t_tbd, t_ud, t_t64, t_ob, tl, tra, trb, free
            free = [(q.sem, q.count) for q in (pe, act, dve, pool)]
            t_tb = dve.do(lambda e: e.tensor_copy(
                TB[:, :, :, :], UB[:, :, :, :].rearrange("p k j a -> p k a j")), box["u"], box["p"])
            s_ub, s_tb = sem("s_ub"), sem("s_tb")
            t_ub = sp.dma(UBD, UB[:, 1, :, :], s_ub, box["u"])
            t_tbd = sp.dma(TBD, TB[:, 0, :, :], s_tb, t_tb)
            sp.wait(t_zero)
            s_ud, s_t64 = sem("s_ud"), sem("s_t64")
            for hf in range(2):
                for k in range(2):
                    o = 64 * hf + 32 * k
                    t_ud = sp.dma(UD[:, o:o + 32, o:o + 32], UB[64 * hf:64 * hf + 64, k, :, :], s_ud, box["u"])
            for k in range(2):
                t_t64 = sp.dma(T64[:, 32 * k:32 * k + 32, 32 * k:32 * k + 32], TB[0:64, k, :, :], s_t64, t_tb)

            t_lb = pool.do(lambda e: e.memset(LB[:, :, :], 0.0), *free)
            t_ob = pool.do(lambda e: e.memset(OB[:, :, :], 0.0), *free)
            s_lb, s_ra, s_rb = sem("s_lb"), sem("s_ra"), sem("s_rb")
            t_nbf = [t_ub, t_ud, t_tb, box["p"]]
            for q in range(4):
                p = slice(32 * q, 32 * q + 32)
                for hf in range(2):
                    tl = sp.dma(LB[p, 16 * hf:16 * hf + 16, 32 * q:32 * q + 32],
                                LTD[q::4, 64 * hf:64 * hf + 32, 64 * hf + 32:64 * hf + 64].rearrange(
                                    "m a b -> a m b"), s_lb, t_lb)
                tra = sp.dma(RA[p, :, :], TBD[q::4].rearrange("m a b -> a m b"), s_ra, t_tbd, *t_nbf)
                trb = sp.dma(RB[p, :, :], UBD[q::4].rearrange("m a b -> a m b"), s_rb, t_ub, *t_nbf)

        st = {}

        def join32():
            ps, f = PSW.take()
            for g in range(32):
                t = pe.do(lambda e: e.matmul(ps[:, 32 * g:32 * g + 32], LB[:, g, :], RA[:, g, :],
                                             start=True, stop=True), tl, tra, *f, mark=g == 31)
            for q in range(4):
                p = slice(32 * q, 32 * q + 32)
                t2 = dve.do(lambda e: e.tensor_copy(
                    OB[p, :, 32 * q:32 * q + 32], ps[p, :].rearrange("p (g c) -> p g c", g=32)), t, t_ob)
            PSW.put(ps, t2)
            st["o"], st["l"] = t2, t

        def join32b():
            ps, f = PSW.take()
            for g in range(32):
                t = pe.do(lambda e: e.matmul(ps[:, 32 * g:32 * g + 32], OB[:, g, :], RB[:, g, :],
                                             start=True, stop=True), st["o"], trb, *f, mark=g == 31)
            X2, XP2 = RA, at(201.3125, [4, 4, 32])
            t3 = act.do(lambda e: e.activation(
                XP2[:, :, :, :], ps[:, 0:512].rearrange("p (n m c) -> p m n c", n=4, m=4), ACT.Copy), t, *free)
            t2 = act.do(lambda e: e.activation(X2[:, :, :].rearrange("p g c -> p (g c)"), ps[:, :],
                                               ACT.Copy), t, st["l"])
            PSW.put(ps, t2)
            st["x"], st["b"], st["xp"] = t3, t, XP2
            s_x = sem("s_t21")
            for q in range(4):
                for hf in range(2):
                    st["ud"] = sp.dma(
                        UD[q::4, 64 * hf:64 * hf + 32, 64 * hf + 32:64 * hf + 64].rearrange("m a b -> a m b"),
                        X2[32 * q:32 * q + 32, 16 * hf:16 * hf + 16, :], s_x, t2)

        def join32c():
            ps, f = PSW.take()
            for m in range(4):
                t = pe.do(lambda e: e.transpose(
                    ps[:, 128 * m:128 * m + 128],
                    st["xp"][:, m, :, :].rearrange("p n c -> p (n c)"), ident[:, :]), st["x"], *f, mark=m == 3)
            X3 = at(185.3125, [4, 4, 32])
            t2 = act.do(lambda e: e.activation(X3[:, :, :, :].rearrange("p m q c -> p (m q c)"),
                                               ps[:, 0:512], ACT.Copy), t, t_ub, t_ud, t_tb)
            PSW.put(ps, t2)
            s_x = sem("s_t21n")
            for m4 in range(4):
                st["t64"] = sp.dma(
                    T64[16 * m4:16 * m4 + 16, 32:64, 0:32].rearrange("n a b -> a n b"),
                    X3[32 * m4:32 * m4 + 32, :, :, :].rearrange("p m q c -> p (m q) c"), s_x, t2)
            st["c"] = t

        def load64():
            fr = [st["ud"], st["t64"], st["b"], st["c"], st["o"]]
            t1 = pool.do(lambda e: e.memset(LB[:, :, :], 0.0), *fr)
            st["ob"] = pool.do(lambda e: e.memset(OB[:, :, :], 0.0), *fr)
            s_l, s_r, s_u = sem("s_l64"), sem("s_r64"), sem("s_u64")
            st["ra"], st["rb"] = at(177.3125, [32, 64]), at(185.3125, [32, 64])
            for q in range(2):
                p = slice(64 * q, 64 * q + 64)
                st["tl"] = sp.dma(LB[p, :, 64 * q:64 * q + 64],
                                  LTD[q::2, 0:64, 64:128].rearrange("m a b -> a m b"), s_l, t1)
                st["tra"] = sp.dma(st["ra"][p, :, :], T64[q::2].rearrange("m a b -> a m b"), s_r,
                                   st["t64"], t_t64, *fr)
                st["trb"] = sp.dma(st["rb"][p, :, :],
                                   UD[q::2, 64:128, 64:128].rearrange("m a b -> a m b"), s_u,
                                   st["ud"], t_ud, *fr)

        def join64(n):
            ps, f = PSW.take()
            for g in range(16):
                t = pe.do(lambda e: e.matmul(ps[:, 64 * g:64 * g + 64], LB[:, 16 * n + g, :],
                                             st["ra"][:, 16 * n + g, :], start=True, stop=True),
                          st["tl"], st["tra"], *f, mark=g == 15)
            for q in range(2):
                p = slice(64 * q, 64 * q + 64)
                t2 = dve.do(lambda e: e.tensor_copy(
                    OB[p, 16 * n:16 * n + 16, 64 * q:64 * q + 64],
                    ps[p, :].rearrange("p (g c) -> p g c", g=16)), t, st["ob"])
            PSW.put(ps, t2)
            st["j", n] = t2

        def join64b(n):
            ps, f = PSW.take()
            for g in range(16):
                t = pe.do(lambda e: e.matmul(ps[:, 64 * g:64 * g + 64], OB[:, 16 * n + g, :],
                                             st["rb"][:, 16 * n + g, :], start=True, stop=True),
                          st["j", n], st["trb"], *f, mark=g == 15)
            x = at(193.3125 + 4 * n, [16, 64])
            t2 = act.do(lambda e: e.activation(x[:, :, :].rearrange("p g c -> p (g c)"), ps[:, :],
                                               ACT.Copy), t, t_tbd, t_t64)
            PSW.put(ps, t2)
            s_x = sem(f"s_t64_{n}")
            for q in range(2):
                st["u", n] = sp.dma(
                    UD[32 * n + q:32 * n + 32:2, 0:64, 64:128].rearrange("m a b -> a m b"),
                    x[64 * q:64 * q + 64, :, :], s_x, t2)

        plan = {n: [lambda n=n: decay(n - 1), lambda n=n: n < 8 and start_decay(n)] for n in range(1, 9)}
        plan[0] = [small_decays]
        later = {8: [norm_k, start_substitution], 17: [start_joins], 20: [join32], 21: [join32b],
                 22: [join32c, load64]}
        for n in range(24):
            if 7 <= n < 15:
                fetch_kt(n - 7)
            follow = lambda: (k_head, q_head, v_head)[(n - 1) // 8]((n - 1) % 8, *ready.pop(n - 1))
            advance(n, n + 8 if n < 8 else n - 8 if n < 16 else n,
                    plan.get(n, []) + ([follow] if n else []))
            if n == 16:
                t_cq = dve.do(lambda e: e.tensor_scalar(ssq[:, :], ssq[:, :], EPS, 128 * EPS,
                                                        op0=ALU.add, op1=ALU.mult), (dve.sem, dve.count))

            W.ql = pool if 8 <= n < 16 else dve
            if n == 16:
                W.q = act
            for fn in later.get(n, []):
                fn()
        s_h = [sem(f"s_hback{m}") for m in range(8)]
        iv1 = at(201.3125, [S])
        STEP = Slots([])
        def load_step(b):
            (bufs, sems), f = STEP.take()
            U_done = [st["u", 0], st["u", 1], st["ud"], t_ud]
            srcs = ((KTD, t_kt), (KDD, t_kd), (QTD, t_qt), (QKT, t_qk), (VPD, t_vp), (None, U_done))
            toks = [None] * 6
            for i in (0, 2, 4, 5, 1, 3):
                src, tk = srcs[i]
                ap = UD[8 * b:8 * b + 8].rearrange("h j i -> j h i") if src is None else src[b]
                toks[i] = sp.dma(bufs[i][:, :, :], ap, sems[i], *f, *tk)
            return bufs, sems, toks

        def load_gate(b):
            (g, s_g), f = GATE.take()
            return g, s_g, sp.dma(g[:, :, :], GTD[b], s_g, *f, *t_gt)

        def step_slot(kb, free):
            STEP.line.append((([at(kb + 4 * k, [8, 128]) for k in range(6)],
                               [sem(f"s_step{kb}_{k}") for k in range(6)]), free))

        t_gt = []
        for h in range(8):
            ps, t_gate = tiles.pop(24) if h == 0 else dense(N2)
            if h == 1:
                v_head(7, *ready.pop(23))
            if h == 2:
                join64(0)
                join64(1)
            if h == 3:
                join64b(0)
                join64b(1)
                for _ in range(8):
                    b, f = TMP.take()
                    if b is tmps[7]:
                        t_tmp7 = f
                    else:
                        TMP.put(b, *f)
                fr = t_tmp7 + [st["j", 0], st["j", 1], st["u", 0], st["u", 1], t, (pe.sem, pe.count)]
                for m in range(KT):
                    t_h[m] = sp.dma(H[:, m, :], HD[m], s_h[m], t_hd[m], *fr)
                t_iv1 = spread(diagonals(ivf, t_f), iv1[:, :], free=fr)
            g, f = TMP.take()
            t = mult(g[:, :], ps[:, :], INV[:, :], t_gate, N2.t_inv, *f)
            PSW.put(ps, t)
            t = act.do(lambda e: e.activation(g[:, :], g[:, :], ACT.Silu), t)
            if h:
                W.done(t_gate)
            t_gt.append(store(GTD[:, :, h, :].rearrange("b p c -> p b c"), g, t))
            if h == 4:
                step_free = [st["u", 0], st["u", 1], st["tra"], st["trb"], (pe.sem, pe.count)]
                for _ in range(7):
                    b, f = TMP.take()
                    if b is tmps[6]:
                        step_free += f
                    else:
                        TMP.put(b, *f)
                step_slot(173.3125, step_free)
                step0 = load_step(0)
            if h > 4:
                for m in ((0, 1, 2), (3, 4, 5), (6, 7))[h - 5]:
                    t_h[m] = dve.do(lambda e: e.scalar_tensor_tensor(
                        H[:, m, :], H[:, m, :], vec[:, 48 + m:49 + m], iv1[:, :],
                        op0=ALU.mult, op1=ALU.mult), t_h[m], t_iv1)
        tmp_free = {tmps.index(b): f for b, f in TMP.line}
        step_slot(32, [t_gate])
        GATE = Slots([])
        for kb in (197.3125, 56):
            GATE.put((at(kb, [8, 128]), sem(f"s_gate{kb}")), t_gate, *step_free)

        SS = Slots([])
        for kb in (60, 64):
            SS.put([at(kb + 0.5 * h, [128]) for h in range(8)], t_gate)
        RV, VN, O1, O2, SQ, YT, YU = (Slots([]) for _ in range(7))
        slots_free = step_free + [(q.sem, q.count) for q in (pe, act)]
        for slots, kb, under in ((VN, 145.25, ()), (RV, 149.25, (0,)), (O1, 153.25, (0, 1)), (O2, 84, ()),
                                 (O2, 92, ()), (SQ, 88, ()), (YT, 201.3125, ())):
            slots.put(at(kb, [8, 128]), *slots_free, *[tok for i in under for tok in tmp_free[i]],
                      *([t_h[7]] if slots is YT else []))
        for kb, under in ((68, ()), (157.25, (1, 2, 3, 4, 5))):
            YU.put((at(kb, [8, 256], F32R), at(kb + 8, [8, 256], F32R)), *slots_free,
                   *[tok for i in under for tok in tmp_free[i]])
        BK = Slots([(ps, n) for ps in psum for n in range(2)])
        BK.line = []
        for ps in psum:
            f = next(f for b, f in PSW.line if b is ps)
            for n in range(2):
                BK.put((ps, n), *f)

        def col(t, b, h):
            return t[:, 8 * b + h:8 * b + h + 1]

        def four(b, g, fn, *after):
            bk, f = BK.take()
            ps = bank(bk)
            for i in range(4):
                l, r = fn(4 * g + i)
                t = pe.do(lambda e: e.matmul(ps[:, 128 * i:128 * i + 128], l, r, start=True, stop=True),
                          *after, *f, mark=i == 3)
            return bk, ps, t

        og = vec[:, 80:81]
        fa, fb, fs = var2, ivf, spl
        steps = {0: step0, 1: load_step(1)}
        gates = {0: load_gate(0), 1: load_gate(1)}
        S_now = None
        y_unit = None
        box = {"f": []}

        def out_begin(m, unit):
            w = W.get()
            bk, f = BK.take()
            out_part(w, bank(bk)[:, 0:256], unit, f)
            return w, bk

        def out_part(w, ps, unit, f=()):
            (wh, wl, th, tl), (yh, yl, t1, t2) = w, unit
            for k in range(8):
                for i, (l, r) in enumerate(((wh, yh), (wl, yh), (wh, yl))):
                    last = k == 7 and i == 2
                    t = pe.do(lambda e: e.matmul(
                        ps, l[:, 128 * k:128 * k + 128], r[:, k, :], start=k == 0 and i == 0, stop=last),
                        *(th + list(f) + t1 if i == 0 else tl + t2), mark=last)
            return t

        def out_end(n, m, w, bk, unit):
            ps = bank(bk)
            t = out_part(w, ps[:, 256:512], unit)
            c = slice(512 * n, 512 * n + 512)
            t_h[m] = dve.do(lambda e: e.tensor_tensor(H[:, m, c], H[:, m, c], ps[:, :], ALU.add),
                            t, t_h[m])
            BK.put(bk, t_h[m])
            W.done(t)
            return t

        def out_half2(n, units, begun=(), order=range(8), hook=None):
            begun = list(begun)
            for m in order:
                t = out_end(n, m, *(begun.pop(0) if begun else out_begin(m, units[0])), units[1])
                if hook:
                    hook(m)
            for yh, yl, _, _ in units:
                YU.put((yh, yl), t)
            units.clear()

        def norm_of(b, o2, t_o2):
            sq, f = SQ.take()
            t = act.do(lambda e: e.activation(sq[:, :, :], o2[:, :, :], ACT.Square), *t_o2, *f)
            c8 = slice(8 * b, 8 * b + 8)

            def rest():
                ts = dve.do(lambda e: e.tensor_reduce(fa[:, 0:8], sq[:, :, :], AX.X, ALU.add), t, *box["f"])
                SQ.put(sq, ts)
                ts = dve.do(lambda e: e.scalar_tensor_tensor(
                    fa[:, 0:8], fa[:, 0:8], 1.0 / 128, ssq[:, c8], op0=ALU.mult, op1=ALU.add), ts, t_cq)
                ts = inv_sqrt(fb[:, 0:8], fa[:, 0:8], fs[:, 0:8], ts)
                t_on = pool.do(lambda e: e.tensor_tensor(
                    o2[:, :, :], o2[:, :, :], fb[:, 0:8].unsqueeze(2).broadcast_to([128, 8, 128]),
                    ALU.mult), ts)
                box["f"] = [t_on]
                late.append(lambda: gated(b, o2, t_on))
            return rest

        def gated(b, o2, t_on):
            if b % 2 == 0:
                box["y"] = YU.take()
                box["t"] = [], []
            y_unit, yf = box["y"]
            Gb, s_g, t_gb = gates.pop(b)
            yt, f = YT.take()
            for g in range(2):
                bk, fk = BK.take()
                ps = bank(bk)
                for i in range(4):
                    t = pe.do(lambda e: e.transpose(ps[:, 128 * i:128 * i + 128],
                                                    o2[:, 4 * g + i, :], ident[:, :]),
                              t_on, *fk, mark=i == 3)
                hs = slice(4 * g, 4 * g + 4)
                t_y = dve.do(lambda e: e.scalar_tensor_tensor(
                    yt[:, hs, :], ps.rearrange("p (h c) -> p h c", h=4), og, Gb[:, hs, :],
                    op0=ALU.mult, op1=ALU.mult), t, t_gb, t_const, *f)
                BK.put(bk, t_y)
            O2.put(o2, t)
            GATE.put((Gb, s_g), t_y)
            if b < 6:
                gates[b + 2] = load_gate(b + 2)
            c = slice(128 * (b % 2), 128 * (b % 2) + 128)
            t1, t2 = split(yt[:, :, :], y_unit[0][:, :, c], y_unit[1][:, :, c], t_y, *yf,
                           ql=pool if b < 5 else dve)
            YT.put(yt, t1, t2)
            box["t"][0].append(t1)
            box["t"][1].append(t2)
            if b % 2:
                units.append((*y_unit, *box["t"]))

        units = []
        late, late_norm = [], []
        for b in range(8):
            bufs, sems, toks = steps.pop(b)
            KTb, KDb, QTb, QKb, VPb, Ub = bufs
            rv, rf = RV.take()
            vn, vf = VN.take()
            o1, o1f = O1.take()
            S_new, sf = SS.take() if b < 7 else (None, [])
            t_s = {}
            ks, x1, xx = {}, {}, {}
            if b:
                for g in range(2):
                    ks[g] = four(b, g, lambda h: (KTb[:, h, :], S_now[0][h][:, :]), toks[0], *S_now[1][g])
                for g in range(2):
                    x1[g] = four(b, g, lambda h: (QTb[:, h, :], S_now[0][h][:, :]), toks[2], *S_now[1][g])
            rest = late_norm.pop(0)() if b else None
            t_r, t_o1 = [toks[4]] * 2, [None] * 2
            if b:
                for g in range(2):
                    bk, ps, t = ks[g]
                    for i in range(4):
                        h = 4 * g + i
                        t_r[g] = dve.do(lambda e: e.scalar_tensor_tensor(
                            rv[:, h, :], ps[:, 128 * i:128 * i + 128], col(eGn, b, h), VPb[:, h, :],
                            op0=ALU.mult, op1=ALU.add), t, toks[4], t_egn, *rf)
                    BK.put(bk, t_r[g])
            src = rv if b else VPb
            if rest:
                rest()
            t_v = [None] * 2
            for g in range(2):
                bk, ps, t = four(b, g, lambda h: (Ub[:, h, :], src[:, h, :]), toks[5], t_r[g])
                for i in range(4):
                    h = 4 * g + i
                    t_v[g] = act.do(lambda e: e.activation(
                        vn[:, h, :], ps[:, 128 * i:128 * i + 128], ACT.Copy, scale=col(bc, b, h)),
                        t, *t_b, *vf)
                BK.put(bk, t_v[g])
            RV.put(rv, t)
            if b:
                for g in range(2):
                    bk1, ps1, t1 = x1[g]
                    for i in range(4):
                        h = 4 * g + i
                        t_o1[g] = act.do(lambda e: e.activation(
                            o1[:, h, :], ps1[:, 128 * i:128 * i + 128], ACT.Copy, scale=col(eG, b, h)),
                            t1, t_eg, *o1f)
                    BK.put(bk1, t_o1[g])
            if b > 1:
                late.pop(0)()
            o2, o2f = O2.take()
            t_sn = [None] * 2
            t_o2 = [None] * 2
            if b < 7:
                for g in range(2):
                    bk, ps, t = four(b, g, lambda h: (KDb[:, h, :], vn[:, h, :]), toks[1], t_v[g])
                    for i in range(4):
                        h = 4 * g + i
                        pb_ = ps[:, 128 * i:128 * i + 128]
                        if b:
                            t_sn[g] = dve.do(lambda e: e.scalar_tensor_tensor(
                                S_new[h][:, :], S_now[0][h][:, :], col(eGL, b, h), pb_,
                                op0=ALU.mult, op1=ALU.add), t, t_eg, *S_now[1][g], *sf)
                        else:
                            t_sn[g] = dve.do(lambda e: e.tensor_copy(S_new[h][:, :], pb_), t, *sf)
                    BK.put(bk, t_sn[g])
            for g in range(2):
                bk, ps, t = four(b, g, lambda h: (QKb[:, h, :], vn[:, h, :]), toks[3], t_v[g])
                hs = slice(4 * g, 4 * g + 4)
                o2g = o2[:, hs, :]
                p3 = ps.rearrange("p (h c) -> p h c", h=4)
                if b:
                    t_o2[g] = dve.do(lambda e: e.tensor_tensor(o2g, p3, o1[:, hs, :], ALU.add),
                                     t, t_o1[g], *o2f)
                else:
                    t_o2[g] = dve.do(lambda e: e.tensor_copy(o2g, p3), t, *o2f)
                BK.put(bk, t_o2[g])
                t_vnf = t
            VN.put(vn, t_vnf)
            O1.put(o1, t_o2[1])
            if S_now:
                SS.put(S_now[0], t_vnf, *[x for x in t_sn if x])
            S_now = (S_new, [[t_sn[0]], [t_sn[1]]]) if b < 7 else None
            STEP.put((bufs, sems), t_vnf)
            if b < 6:
                steps[b + 2] = load_step(b + 2)
            late_norm.append(lambda b=b, o2=o2, t_o2=t_o2: norm_of(b, o2, t_o2))
            if b == 5:
                out_half2(0, units)
        rest = late_norm.pop(0)()
        begun = [out_begin(m, units[0]) for m in LAST[:2]]
        rest()
        late.pop(0)()
        begun.append(out_begin(LAST[2], units[0]))
        late.pop(0)()

        end = [(q.sem, q.count) for q in (pe, act, dve, pool)]
        ACC = [at(139 + 4 * i, [S]) for i in range(8)]
        TMP = Slots([])
        for b in [at(203, [S])] + ACC[0:4]:
            TMP.put(b, *end)
        N3 = Norm(vec[:, 64:72])

        def feed4(m):
            N3.high(m, t_h[m], *end)
            if m in LAST[:4]:
                N3.low(m, t_h[m], *end)
            N3.sq.feed(m, H[:, m, :], t_h[m])

        out_half2(1, units, begun, LAST, feed4)
        end = [(q.sem, q.count) for q in (pe, act, dve, pool)]
        for m in LAST[4:]:
            N3.low(m, t_h[m], *end)

        PSW = Slots([])
        for ps in psum:
            PSW.put(ps, *[tok for (b, _), f in BK.line if b is ps for tok in f])
        for b in ACC[4:]:
            TMP.put(b, *end)
        RH = [at(171 + 8 * i, [S], F32R) for i in range(4)]
        RL = [at(175 + 8 * i, [S], F32R) for i in range(4)]

        def square_relu(ps, t, i, *free):
            r, f = TMP.take()
            t = act.do(lambda e: e.activation(r[:, :], ps[:, :], ACT.Relu), t, *f)
            PSW.put(ps, t)
            t = act.do(lambda e: e.activation(r[:, :], r[:, :], ACT.Square), t)
            t1, t2 = split(r[:, :], RH[i][:, :], RL[i][:, :], t, *free)
            TMP.put(r, t1, t2)
            return [t1], [t2]

        pair = dense_pair(N3, ks=LAST)
        rs = [None] * 4
        for i in range(2):
            W.done(pair[i][1])
            rs[i] = square_relu(*pair[i], i, *end)
        ps2, t = dense(N3)
        W.done(t)
        rs[2] = square_relu(ps2, t, 2, *end)
        ps, f = PSW.take()
        t = mean_eps(var[:, :], ps[:, 0:8], N3.sq.columns(ps, f))
        PSW.put(ps, t)
        t_inv1 = dve.do(lambda e: e.reciprocal(invc[:, :], var[:, :]), t)
        ps2, t = dense(N3)
        W.done(t)
        rs[3] = square_relu(ps2, t, 3, *end)
        acc_free = [tok for _, f in TMP.line for tok in f]
        TMP.line = [(b, f) for b, f in TMP.line if b not in ACC]
        dg2 = diagonals(invc, t_inv1)
        t_acc = [acc_free] * 8
        for g in range(7):
            for i in range(4):
                if rs[i] is None:
                    ps, t = dense(N3)
                    W.done(t)
                    rs[i] = square_relu(ps, t, i, *rfree) if g else square_relu(ps, t, i, *end)
            ahead = dense(N3)
            W.done(ahead[1])
            for j in range(4):
                wh, wl, th, tl = W.get()
                for x in range(2):
                    m = 2 * j + x
                    ps, free = PSW.take()
                    o = 512 * x
                    t = product(ps, [(wh[:, o + 128 * k:o + 128 * k + 128], wl[:, o + 128 * k:o + 128 * k + 128],
                                      RH[k], RL[k], th + rs[k][0] + free, tl + rs[k][1])
                                     for k in range(4)])
                    if g == 0:
                        t_acc[m] = [act.do(lambda e: e.activation(ACC[m][:, :], ps[:, :], ACT.Copy),
                                           t, *t_acc[m])]
                    else:
                        t_acc[m] = [dve.do(lambda e: e.tensor_tensor(
                            ACC[m][:, :], ACC[m][:, :], ps[:, :], ALU.add), t, *t_acc[m])]
                    PSW.put(ps, *t_acc[m])
                W.done(t)
                if g == 0 and j == 0:
                    t_inv2 = spread(dg2, INV[:, :])
            rfree = [t]
            rs = [None] * 4
            rs[0] = square_relu(*ahead, 0, *rfree)

        def settle(*ms):
            for m in ms:
                ta = mult(ACC[m][:, :], ACC[m][:, :], INV[:, :], *t_acc[m], t_inv2)
                t_h[m] = dve.do(lambda e: e.tensor_tensor(H[:, m, :], H[:, m, :], ACC[m][:, :],
                                                          ALU.add), ta, t_h[m])

        settle(0)
        for i, before, behind in ((1, (1,), (2, 3)), (2, (4,), (5, 6)), (3, (7,), ())):
            ps, t = dense(N3)
            W.done(t)
            settle(*before)
            rs[i] = square_relu(ps, t, i, *rfree)
            settle(*behind)
        t_ufree = t
        ws = [W.get() for _ in range(3)]
        w3 = at(32, [S], F32R), at(36, [S], F32R)
        SQ2 = Slots([])
        for i in range(4):
            SQ2.put(at(64 + 2 * i, [512]), t_ufree)
        TH = Slots([])
        for i in range(2):
            TH.put(at(72 + 2 * i, [512]), t_ufree)
        DG = at(76, [4, 128])
        BK = Slots([])
        for ps, f in PSW.line:
            for n in range(2):
                BK.put((ps, n), *f)
        s_out = [sem(f"s_out{m}") for m in range(8)]
        outs = []

        class Half:
            def __init__(self, n):
                self.n, self.c, self.acc = n, slice(512 * n, 512 * n + 512), None

            def tile(self, m):
                self.end(m, self.begin(m))

            def begin(self, m, k0=0, k1=4, slot=None):
                wh, wl, th, tl = ws[m // 2]
                bk, free, _ = slot or (*BK.take(), None)
                ps, c, o = bank(bk), self.c, 512 * (m % 2)
                for k in range(k0, k1):
                    w = slice(o + 128 * k, o + 128 * k + 128)
                    for i, (l, r) in enumerate(((wh, RH[k]), (wl, RH[k]), (wh, RL[k]))):
                        last = k == 3 and i == 2
                        t = pe.do(lambda e: e.matmul(ps, l[:, w], r[:, c], start=k == 0 and i == 0, stop=last),
                                  *(th + rs[k][0] + free if i == 0 else tl + rs[k][1]), mark=last)
                return bk, free, t

            def end(self, m, slot):
                bk, _, t = slot
                ps, c = bank(bk), self.c
                d, f = TH.take()
                t = mult(d[:, :], ps, INV[:, c], t, t_inv2, *f)
                BK.put(bk, t)
                t_h[m] = dve.do(lambda e: e.tensor_tensor(H[:, m, c], H[:, m, c], d[:, :], ALU.add),
                                t, t_h[m])
                TH.put(d, t_h[m])
                sq, f = SQ2.take()
                t = act.do(lambda e: e.activation(sq[:, :], H[:, m, c], ACT.Square), t_h[m], *f)
                if self.acc is None:
                    self.acc, self.t = sq, t
                else:
                    q = dve if self.n and m == 7 else pool
                    self.t = q.do(lambda e: e.tensor_tensor(
                        self.acc[:, :], self.acc[:, :], sq[:, :], ALU.add), t, self.t)
                    SQ2.put(sq, self.t)

            def root(self):
                bk, f = BK.take()
                ps = bank(bk)
                for j in range(4):
                    t = pe.do(lambda e: e.matmul(
                        ps[:, j:j + 1], self.acc[:, 128 * j:128 * j + 128], ones[:, 0:1],
                        start=True, stop=True), self.t, t_ones, *f, mark=j == 3)
                SQ2.put(self.acc, t)
                c = slice(4 * self.n, 4 * self.n + 4)
                t = mean_eps(var[:, c], ps[:, 0:4], t)
                BK.put(bk, t)
                t = inv_sqrt(invc[:, c], var[:, c], sd[:, c], t)
                self.t = dve.do(lambda e: e.tensor_tensor(
                    DG[:, :, :], ident[:, :].unsqueeze(1).broadcast_to([128, 4, 128]),
                    invc[:, c].unsqueeze(2).broadcast_to([128, 4, 128]), ALU.mult),
                    t, t_ident, t_ufree, *dg_free)

            def spread(self):
                bk, f = BK.take()
                self.inv = bank(bk)
                self.t_inv = pe.do(lambda e: e.matmul(
                    self.inv, ones[:, :], DG[:, :, :].rearrange("p b c -> p (b c)"), start=True,
                    stop=True), self.t, t_ones, *f)
                dg_free.append(self.t_inv)

            def write(self, m):
                t = dve.do(lambda e: e.scalar_tensor_tensor(
                    H[:, m, self.c], H[:, m, self.c], vec[:, 72 + m:73 + m], self.inv,
                    op0=ALU.mult, op1=ALU.mult), self.t_inv, t_h[m])
                outs.append(sp.dma(out[128 * m:128 * m + 128, self.c], H[:, m, self.c], s_out[m], t))

        dg_free = []
        a, b = Half(0), Half(1)
        for m in range(8):
            if m == 2:
                ws.append((*w3, *W.split_into(*w3, t_ufree)))
            if m == 0:
                pair = [a.begin(x, 0, 3) for x in range(2)]
            if m < 2:
                a.end(m, a.begin(m, 3, 4, pair[m]))
            else:
                a.tile(m)
        for m in range(8):
            if m == 2:
                a.root()
            if m == 3:
                a.spread()
            b.tile(m)
            if 3 < m < 7:
                a.write(2 * m - 8)
                a.write(2 * m - 7)
        b.root()
        b.spread()
        a.write(6)
        a.write(7)
        for m in range(8):
            b.write(m)
        sp.wait(*outs)


def lay_out(inputs):
    def tiles(w, kb, mb):
        k, m = w.shape
        t = w.reshape(k // (128 * kb), kb, 128, m // (128 * mb), mb, 128)
        return np.ascontiguousarray(t.transpose(0, 3, 2, 4, 1, 5)).reshape(-1, 128, 1024)

    def cols(v):
        return v.reshape(-1, 128).T

    f = {k: np.asarray(v) for k, v in inputs.items()}
    count = 1.0 / np.arange(1, 17, dtype=np.float32)
    A = {
        "xT": np.ascontiguousarray(f["x"][0].T),
        "ident": np.eye(128, dtype=np.float32),
        "vec": np.ascontiguousarray(np.concatenate([
            cols(f["norm_g"][0]), np.broadcast_to(count, (128, 16)), cols(f["pool_scale"][0]),
            cols(f["norm_g"][1]), cols(f["norm_f"]), cols(f["norm_mix_g_2"][0]),
            cols(f["norm_mlp_g_2"][0]), cols(f["final_norm_g_2"]), cols(f["gdn_o_norm_g_2"][0]),
        ], axis=1)),
        "pool_in": tiles(f["pool_w_in"][0], 8, 1),
        "pool_g": np.concatenate([tiles(f["pool_w"][0, g], 4, 2) for g in range(4)]),
        "pool_out": tiles(f["pool_w_out"][0], 2, 4),
    }
    A["sb_in"] = tiles(f["sb_w_in"][0], 8, 1)
    wv = f["sb_w_in"][0][:, 2048:4096].reshape(4, 2, 128, 4, 512)
    A["sb_v"] = np.ascontiguousarray(wv.transpose(3, 0, 2, 1, 4)).reshape(16, 128, 1024)
    A["sb_out"] = tiles(f["sb_w_out"][0], 2, 4)
    mask = np.where(np.arange(128)[None, :] < np.arange(128)[:, None], 0.0, -1e30)
    A["mask"] = mask.astype(np.float32)
    i = np.arange(128)
    A["tri_incl"] = (i[:, None] <= i[None, :]).astype(np.float32)
    A["tri_strict"] = (i[:, None] > i[None, :]).astype(np.float32)
    gw = f["gdn_w_in_2"][0]
    A["gdn_in"] = tiles(np.ascontiguousarray(gw[:, 0:4096]), 8, 1)
    A["gdn_ab"] = np.ascontiguousarray(gw[:, 4096:4112].reshape(8, 128, 16).transpose(1, 0, 2)).reshape(128, 128)
    A["gdn_vec"] = np.ascontiguousarray(np.concatenate([
        f["gdn_conv_w_2"][0].reshape(4, 24, 128).transpose(2, 1, 0).reshape(128, 96),
        np.broadcast_to(f["gdn_a_log_2"][0], (128, 8)), np.broadcast_to(f["gdn_dt_bias_2"][0], (128, 8)),
    ], axis=1))
    A["gdn_out"] = tiles(f["gdn_w_out_2"][0], 8, 1)
    A["w1"] = tiles(f["mlp_w1_2"][0], 8, 1)
    A["w2"] = tiles(f["mlp_w2_2"][0], 4, 2)
    return A


def kernel(**inputs):
    import concourse.bacc as bacc
    from concourse.bass_utils import run_bass_kernel_spmd

    A = lay_out(inputs)
    nc = bacc.Bacc("TRN2", target_bir_lowering=False, num_devices=1)
    args = {k: nc.dram_tensor("in_" + k, v.shape, mybir.dt.from_np(v.dtype), kind="ExternalInput").ap()
            for k, v in A.items()}
    out = nc.dram_tensor("out", (D, S), F32, kind="ExternalOutput").ap()
    program(nc, args, out)
    r = run_bass_kernel_spmd(nc, [{"in_" + k: v for k, v in A.items()}], core_ids=[0])
    return np.ascontiguousarray(r.results[0]["out"].T)[None]
```
